# Optimizing a Trainium2 kernel written in Bass

```python
import math
import jax, jax.numpy as jnp
from jax import lax
import numpy as np

D_MODEL = 1024
BATCH = 1
SEQ = 256
DEPTH = 2

N_A_LAYERS = DEPTH // 2
N_B_LAYERS = DEPTH - N_A_LAYERS

A_CHUNK = 128
A_GROUPS = 8
A_WIDTH = 2 * D_MODEL
A_GROUP_DIM = A_WIDTH // A_GROUPS

B_HEADS = 16
B_HEAD_DIM = D_MODEL // B_HEADS
B_BLOCK = 256
B_TOPK = 3
B_QCHUNK = 32

N_EXPERTS = 64
TOP_K = 8
N_GROUPS = 8
TOPK_GROUPS = 4
EXPERT_DIM = 256
SHARED_DIM = 256
ROUTED_SCALE = 2.5
MOE_ROW_BLOCK = 128

RMS_EPS = 1e-6
LN_EPS = 1e-5
NEG_INF = -1e30


def rmsnorm(x, g):
    xf = x.astype(jnp.float32)
    y = xf * lax.rsqrt(jnp.mean(xf * xf, axis=-1, keepdims=True) + RMS_EPS)
    return y.astype(x.dtype) * g

def layernorm(x, g, b):
    xf = x.astype(jnp.float32)
    mu = jnp.mean(xf, axis=-1, keepdims=True)
    var = jnp.mean(jnp.square(xf - mu), axis=-1, keepdims=True)
    y = (xf - mu) * lax.rsqrt(var + LN_EPS)
    return y.astype(x.dtype) * g + b

def ada(c, w, b, n):
    m = jax.nn.silu(c) @ w + b
    return [t[:, None, :] for t in jnp.split(m, n, axis=-1)]

def modulate(h, shift, scale):
    return h * (1 + scale) + shift

def swiglu(x, wg, wu, wd):
    return (jax.nn.silu(x @ wg) * (x @ wu)) @ wd

def gmlp_mixer(h, w_in, b_in, ln_g, ln_b, w_s, b_s, w_out):
    B, S, _ = h.shape
    z = jax.nn.gelu(h @ w_in + b_in)
    u, v = jnp.split(z, 2, axis=-1)
    v = layernorm(v, ln_g, ln_b)
    nc = S // A_CHUNK
    v = v.reshape(B, nc, A_CHUNK, A_GROUPS, A_GROUP_DIM)
    causal = jnp.tril(jnp.ones((A_CHUNK, A_CHUNK), dtype=bool))
    w = jnp.where(causal[None], w_s, 0)
    sv = jnp.einsum('gts,bcsgd->bctgd', w, v) + b_s.T[None, None, :, :, None]
    y = u * sv.reshape(B, S, A_WIDTH)
    return y @ w_out

def shared_kv(x, c, g, w_ada, b_ada, w_k, w_v):
    shift, scale = ada(c, w_ada, b_ada, 2)
    h = modulate(rmsnorm(x, g), shift, scale)
    B, S, _ = h.shape
    k = (h @ w_k).reshape(B, S, B_HEADS, B_HEAD_DIM).transpose(0, 2, 1, 3)
    v = (h @ w_v).reshape(B, S, B_HEADS, B_HEAD_DIM).transpose(0, 2, 1, 3)
    nb = -(-S // B_BLOCK)
    pad = nb * B_BLOCK - S
    k = jnp.pad(k, ((0, 0), (0, 0), (0, pad), (0, 0)))
    v = jnp.pad(v, ((0, 0), (0, 0), (0, pad), (0, 0)))
    kb = k.reshape(B, B_HEADS, nb, B_BLOCK, B_HEAD_DIM)
    vb = v.reshape(B, B_HEADS, nb, B_BLOCK, B_HEAD_DIM)
    kmean = jnp.mean(kb, axis=3)
    return kb, vb, kmean

def moba_attention(q, kb, vb, kmean):
    B, H, S, dh = q.shape
    nb = kb.shape[2]
    n_sel = min(B_TOPK, nb - 1)
    scale = dh ** -0.5
    nqc = S // B_QCHUNK
    qc = q.reshape(B, H, nqc, B_QCHUNK, dh).transpose(0, 2, 1, 3, 4)
    head_idx = jnp.arange(H)[:, None, None]

    def one_seq(args):
        q_s, kb_s, vb_s, km_s = args

        def one_chunk(args2):
            ci, q_c = args2
            start = ci * B_QCHUNK
            own = start // B_BLOCK
            qpos = start + jnp.arange(B_QCHUNK)
            kpos = own * B_BLOCK + jnp.arange(B_BLOCK)
            k_own = lax.dynamic_index_in_dim(kb_s, own, axis=1, keepdims=False)
            v_own = lax.dynamic_index_in_dim(vb_s, own, axis=1, keepdims=False)
            s_own = jnp.einsum('hqd,hjd->hqj', q_c, k_own).astype(jnp.float32) * scale
            s_own = jnp.where((kpos[None, :] <= qpos[:, None])[None], s_own, NEG_INF)
            if n_sel > 0:
                gate = jnp.einsum('hqd,hnd->hqn', q_c, km_s).astype(jnp.float32)
                past = jnp.arange(nb) < own
                gate = jnp.where(past[None, None, :], gate, NEG_INF)
                _, idx = lax.top_k(gate, n_sel)
                valid = idx < own
                k_sel = kb_s[head_idx, idx]
                v_sel = vb_s[head_idx, idx]
                s_sel = jnp.einsum('hqd,hqnjd->hqnj', q_c, k_sel).astype(jnp.float32) * scale
                s_sel = jnp.where(valid[..., None], s_sel, NEG_INF)
                s = jnp.concatenate([s_sel.reshape(H, B_QCHUNK, n_sel * B_BLOCK), s_own], axis=-1)
                p = jax.nn.softmax(s, axis=-1).astype(v_own.dtype)
                p_sel = p[..., :n_sel * B_BLOCK].reshape(H, B_QCHUNK, n_sel, B_BLOCK)
                p_own = p[..., n_sel * B_BLOCK:]
                o = (jnp.einsum('hqnj,hqnjd->hqd', p_sel, v_sel)
                     + jnp.einsum('hqj,hjd->hqd', p_own, v_own))
            else:
                p = jax.nn.softmax(s_own, axis=-1).astype(v_own.dtype)
                o = jnp.einsum('hqj,hjd->hqd', p, v_own)
            return o

        return lax.map(one_chunk, (jnp.arange(nqc), q_s))

    o = lax.map(one_seq, (qc, kb, vb, kmean))
    return o.transpose(0, 2, 1, 3, 4).reshape(B, H, S, dh)

def moba_mixer(h, w_q, w_o, kb, vb, kmean):
    B, S, D = h.shape
    q = (h @ w_q).reshape(B, S, B_HEADS, B_HEAD_DIM).transpose(0, 2, 1, 3)
    o = moba_attention(q, kb, vb, kmean)
    return o.transpose(0, 2, 1, 3).reshape(B, S, D) @ w_o

def grouped_experts(xt, eidx, w, w_gate, w_up, w_down):
    T, D = xt.shape
    K = eidx.shape[1]
    E, M = N_EXPERTS, MOE_ROW_BLOCK
    TK = T * K
    e_flat = eidx.reshape(TK)
    tok_flat = jnp.arange(TK, dtype=jnp.int32) // K
    w_flat = w.reshape(TK)
    order = jnp.argsort(e_flat)
    e_sorted = e_flat[order]
    tok_sorted = tok_flat[order]
    w_sorted = w_flat[order]
    counts = jnp.zeros((E,), jnp.int32).at[e_flat].add(1)
    starts = jnp.cumsum(counts) - counts
    padded = ((counts + M - 1) // M) * M
    pad_ends = jnp.cumsum(padded)
    pad_starts = pad_ends - padded
    rank = jnp.arange(TK, dtype=jnp.int32) - starts[e_sorted]
    dest = pad_starts[e_sorted] + rank
    n_blocks = -(-(TK + E * (M - 1)) // M)
    R = n_blocks * M
    x_pad = jnp.zeros((R, D), xt.dtype).at[dest].set(xt[tok_sorted])
    block_start = jnp.arange(n_blocks, dtype=jnp.int32) * M
    block_expert = jnp.minimum(jnp.sum(pad_ends[None, :] <= block_start[:, None], axis=1), E - 1)

    def run_block(args):
        xb, e = args
        return swiglu(xb, w_gate[e], w_up[e], w_down[e])

    y_pad = lax.map(run_block, (x_pad.reshape(n_blocks, M, D), block_expert)).reshape(R, D)
    y = y_pad[dest] * w_sorted[:, None].astype(xt.dtype)
    return jax.ops.segment_sum(y, tok_sorted, num_segments=T)

def moe(h, w_router, e_bias, w_gate, w_up, w_down, ws_gate, ws_up, ws_down):
    B, S, D = h.shape
    T = B * S
    xt = h.reshape(T, D)
    scores = jax.nn.sigmoid((xt @ w_router).astype(jnp.float32))
    choice = scores + e_bias.astype(jnp.float32)
    grp = choice.reshape(T, N_GROUPS, N_EXPERTS // N_GROUPS)
    grp_score = jnp.sum(lax.top_k(grp, 2)[0], axis=-1)
    _, gidx = lax.top_k(grp_score, TOPK_GROUPS)
    gmask = jnp.sum(jax.nn.one_hot(gidx, N_GROUPS, dtype=jnp.float32), axis=1) > 0
    emask = jnp.repeat(gmask, N_EXPERTS // N_GROUPS, axis=1)
    choice = jnp.where(emask, choice, NEG_INF)
    _, eidx = lax.top_k(choice, TOP_K)
    w = jnp.take_along_axis(scores, eidx, axis=1)
    w = w / jnp.sum(w, axis=-1, keepdims=True) * ROUTED_SCALE
    routed = grouped_experts(xt, eidx, w, w_gate, w_up, w_down)
    shared = swiglu(xt, ws_gate, ws_up, ws_down)
    return (routed + shared).reshape(B, S, D)

def first_inputs(seed: int = 0) -> dict:
    key = jax.random.key(seed)
    ks = jax.random.split(key, 32)
    f32 = jnp.float32

    def nrm(k, shape, s):
        return jax.random.normal(k, shape, f32) * s

    D = D_MODEL
    return {
        'x': nrm(ks[0], (BATCH, SEQ, D), 1.0),
        'c': nrm(ks[1], (BATCH, D), 1.0),
        'ada_w': nrm(ks[2], (DEPTH, D, 6 * D), 0.2 * D ** -0.5),
        'ada_b': nrm(ks[3], (DEPTH, 6 * D), 0.02),
        'norm_mix': 1.0 + nrm(ks[4], (DEPTH, D), 0.02),
        'norm_ffn': 1.0 + nrm(ks[5], (DEPTH, D), 0.02),
        'a_w_in': nrm(ks[6], (N_A_LAYERS, D, 2 * A_WIDTH), D ** -0.5),
        'a_b_in': nrm(ks[7], (N_A_LAYERS, 2 * A_WIDTH), 0.02),
        'a_ln_g': 1.0 + nrm(ks[8], (N_A_LAYERS, A_WIDTH), 0.02),
        'a_ln_b': nrm(ks[9], (N_A_LAYERS, A_WIDTH), 0.02),
        'a_w_s': nrm(ks[10], (N_A_LAYERS, A_GROUPS, A_CHUNK, A_CHUNK), 0.5 * A_CHUNK ** -0.5),
        'a_b_s': 1.0 + nrm(ks[11], (N_A_LAYERS, A_GROUPS, A_CHUNK), 0.02),
        'a_w_out': nrm(ks[12], (N_A_LAYERS, A_WIDTH, D), A_WIDTH ** -0.5),
        'kv_norm': 1.0 + nrm(ks[13], (D,), 0.02),
        'kv_ada_w': nrm(ks[14], (D, 2 * D), 0.2 * D ** -0.5),
        'kv_ada_b': nrm(ks[15], (2 * D,), 0.02),
        'kv_w_k': nrm(ks[16], (D, D), D ** -0.5),
        'kv_w_v': nrm(ks[17], (D, D), D ** -0.5),
        'b_w_q': nrm(ks[18], (N_B_LAYERS, D, D), D ** -0.5),
        'b_w_o': nrm(ks[19], (N_B_LAYERS, D, D), D ** -0.5),
        'moe_router': nrm(ks[20], (DEPTH, D, N_EXPERTS), D ** -0.5),
        'moe_bias': nrm(ks[21], (DEPTH, N_EXPERTS), 0.01),
        'moe_w_gate': nrm(ks[22], (DEPTH, N_EXPERTS, D, EXPERT_DIM), D ** -0.5),
        'moe_w_up': nrm(ks[23], (DEPTH, N_EXPERTS, D, EXPERT_DIM), D ** -0.5),
        'moe_w_down': nrm(ks[24], (DEPTH, N_EXPERTS, EXPERT_DIM, D), EXPERT_DIM ** -0.5),
        'sh_w_gate': nrm(ks[25], (DEPTH, D, SHARED_DIM), D ** -0.5),
        'sh_w_up': nrm(ks[26], (DEPTH, D, SHARED_DIM), D ** -0.5),
        'sh_w_down': nrm(ks[27], (DEPTH, SHARED_DIM, D), SHARED_DIM ** -0.5),
        'final_norm': 1.0 + nrm(ks[28], (D,), 0.02),
    }

def first_block(x, c, ada_w, ada_b, norm_mix, norm_ffn, a_w_in, a_b_in, a_ln_g, a_ln_b,
              a_w_s, a_b_s, a_w_out, kv_norm, kv_ada_w, kv_ada_b, kv_w_k, kv_w_v,
              b_w_q, b_w_o, moe_router, moe_bias, moe_w_gate, moe_w_up, moe_w_down,
              sh_w_gate, sh_w_up, sh_w_down, final_norm):
    kv = None
    for i in range(DEPTH):
        sh1, sc1, g1, sh2, sc2, g2 = ada(c, ada_w[i], ada_b[i], 6)
        h = modulate(rmsnorm(x, norm_mix[i]), sh1, sc1)
        if i < N_A_LAYERS:
            y = gmlp_mixer(h, a_w_in[i], a_b_in[i], a_ln_g[i], a_ln_b[i],
                           a_w_s[i], a_b_s[i], a_w_out[i])
        else:
            if kv is None:
                kv = shared_kv(x, c, kv_norm, kv_ada_w, kv_ada_b, kv_w_k, kv_w_v)
            j = i - N_A_LAYERS
            y = moba_mixer(h, b_w_q[j], b_w_o[j], kv[0], kv[1], kv[2])
        x = x + g1 * y
        h = modulate(rmsnorm(x, norm_ffn[i]), sh2, sc2)
        x = x + g2 * moe(h, moe_router[i], moe_bias[i], moe_w_gate[i], moe_w_up[i],
                         moe_w_down[i], sh_w_gate[i], sh_w_up[i], sh_w_down[i])
    return rmsnorm(x, final_norm)


POOL_GROUPS = 4
POOL_GROUP_DIM = 128
POOL_WIDTH = POOL_GROUPS * POOL_GROUP_DIM
POOL_WINDOWS = (2, 4, 8, 16)
LRU_HEADS = 10
LRU_HEAD_DIM = 128
LRU_WIDTH = LRU_HEADS * LRU_HEAD_DIM
CONV_WIDTH = 4
LRU_C = 8.0
D_FF = 2816
EPS = 1e-6
IN_WIDTH = POOL_WIDTH + 2 * LRU_WIDTH + 2 * D_MODEL


def rmsnorm_2(x, g):
    xf = x.astype(jnp.float32)
    var = jnp.mean(xf * xf, axis=-1, keepdims=True)
    return (xf * lax.rsqrt(var + EPS) * g.astype(jnp.float32)).astype(x.dtype)

def swiglu_ffn(h, w_up, w_down):
    u = h @ w_up
    a, b = jnp.split(u, 2, axis=-1)
    return (jax.nn.silu(a) * b) @ w_down

def causal_pool_minus_self(u, window):
    b, s, c = u.shape
    uf = u.astype(jnp.float32)
    cs = jnp.cumsum(uf, axis=1)
    cs_pad = jnp.concatenate([jnp.zeros((b, 1, c), jnp.float32), cs], axis=1)
    prev = jnp.concatenate([jnp.zeros((b, window - 1, c), jnp.float32), cs_pad[:, : s - window + 1]], axis=1)
    count = jnp.minimum(jnp.arange(1, s + 1, dtype=jnp.float32), float(window))[None, :, None]
    return ((cs - prev) / count - uf).astype(u.dtype)

def pool_mixer(u, w_grp, b_grp, scale):
    b, s, _ = u.shape
    ug = u.reshape(b, s, POOL_GROUPS, POOL_GROUP_DIM)
    pooled = jnp.stack([causal_pool_minus_self(ug[:, :, g], POOL_WINDOWS[g]) for g in range(POOL_GROUPS)], axis=2)
    mixed = jnp.einsum('bsgc,gcd->bsgd', pooled, w_grp) + b_grp
    return mixed.reshape(b, s, POOL_WIDTH) * scale

def causal_depthwise_conv(u, w, bias):
    s = u.shape[1]
    up = jnp.pad(u, ((0, 0), (CONV_WIDTH - 1, 0), (0, 0)))
    y = sum(up[:, k:k + s] * w[k] for k in range(CONV_WIDTH))
    return y + bias

def _lru_combine(left, right):
    a_l, b_l = left
    a_r, b_r = right
    return a_l * a_r, a_r * b_l + b_r

def rg_lru(u, w_a, b_a, w_x, b_x, lam):
    b, s, _ = u.shape
    uh = u.reshape(b, s, LRU_HEADS, LRU_HEAD_DIM)
    r = jax.nn.sigmoid(jnp.einsum('bshd,hde->bshe', uh, w_a) + b_a).reshape(b, s, LRU_WIDTH)
    i = jax.nn.sigmoid(jnp.einsum('bshd,hde->bshe', uh, w_x) + b_x).reshape(b, s, LRU_WIDTH)
    log_a = -LRU_C * r.astype(jnp.float32) * jax.nn.softplus(-lam.astype(jnp.float32))
    a = jnp.exp(log_a)
    mult = jnp.sqrt(-jnp.expm1(2.0 * log_a))
    bx = mult * (i * u).astype(jnp.float32)
    _, h = lax.associative_scan(_lru_combine, (a, bx), axis=1)
    return h.astype(u.dtype)

def hybrid_mixer(h, w_in, pool_w, pool_b, pool_scale, w_pool_up, conv_w, conv_b,
                 lru_w_a, lru_b_a, lru_w_x, lru_b_x, lru_lambda, w_lru_up, w_out):
    proj = h @ w_in
    s1 = POOL_WIDTH
    s2 = s1 + LRU_WIDTH
    s3 = s2 + LRU_WIDTH
    u_pool, u_lru, u_gelu, g_logits = proj[..., :s1], proj[..., s1:s2], proj[..., s2:s3], proj[..., s3:]
    y_pool = pool_mixer(u_pool, pool_w, pool_b, pool_scale) @ w_pool_up
    v = causal_depthwise_conv(u_lru, conv_w, conv_b)
    y_lru = (rg_lru(v, lru_w_a, lru_b_a, lru_w_x, lru_b_x, lru_lambda) * jax.nn.gelu(u_gelu)) @ w_lru_up
    g = jax.nn.sigmoid(g_logits)
    g_pool, g_lru = g[..., :D_MODEL], g[..., D_MODEL:]
    return (g_pool * y_pool + g_lru * y_lru) @ w_out

def second_inputs(seed: int = 0) -> dict:
    key = jax.random.key(seed)
    ks = jax.random.split(key, 26)
    f32 = jnp.float32

    def nrm(k, shape, fan_in):
        return jax.random.normal(k, shape, f32) * (fan_in ** -0.5)

    def gain(k, shape):
        return 1.0 + 0.02 * jax.random.normal(k, shape, f32)

    def small(k, shape):
        return 0.01 * jax.random.normal(k, shape, f32)

    L = DEPTH
    a_c = jax.random.uniform(ks[17], (L, LRU_WIDTH), f32, 0.9, 0.999)
    sig = a_c ** (1.0 / LRU_C)
    lam = jnp.log(sig) - jnp.log1p(-sig)
    return {
        "x": jax.random.normal(ks[0], (BATCH, SEQ, D_MODEL), f32),
        "norm_ffn1": gain(ks[1], (L, D_MODEL)),
        "ffn1_w_up": nrm(ks[2], (L, D_MODEL, 2 * D_FF), D_MODEL),
        "ffn1_w_down": nrm(ks[3], (L, D_FF, D_MODEL), D_FF),
        "norm_mix": gain(ks[4], (L, D_MODEL)),
        "w_in": nrm(ks[5], (L, D_MODEL, IN_WIDTH), D_MODEL),
        "pool_w": nrm(ks[6], (L, POOL_GROUPS, POOL_GROUP_DIM, POOL_GROUP_DIM), POOL_GROUP_DIM),
        "pool_b": small(ks[7], (L, POOL_GROUPS, POOL_GROUP_DIM)),
        "pool_scale": 1.0 + 0.1 * jax.random.normal(ks[8], (L, POOL_WIDTH), f32),
        "w_pool_up": nrm(ks[9], (L, POOL_WIDTH, D_MODEL), POOL_WIDTH),
        "conv_w": nrm(ks[10], (L, CONV_WIDTH, LRU_WIDTH), CONV_WIDTH),
        "conv_b": small(ks[11], (L, LRU_WIDTH)),
        "lru_w_a": nrm(ks[12], (L, LRU_HEADS, LRU_HEAD_DIM, LRU_HEAD_DIM), LRU_HEAD_DIM),
        "lru_b_a": small(ks[13], (L, LRU_HEADS, LRU_HEAD_DIM)),
        "lru_w_x": nrm(ks[14], (L, LRU_HEADS, LRU_HEAD_DIM, LRU_HEAD_DIM), LRU_HEAD_DIM),
        "lru_b_x": small(ks[15], (L, LRU_HEADS, LRU_HEAD_DIM)),
        "lru_lambda": lam,
        "w_lru_up": nrm(ks[16], (L, LRU_WIDTH, D_MODEL), LRU_WIDTH),
        "w_out": nrm(ks[18], (L, D_MODEL, D_MODEL), D_MODEL),
        "norm_ffn2": gain(ks[19], (L, D_MODEL)),
        "ffn2_w_up": nrm(ks[20], (L, D_MODEL, 2 * D_FF), D_MODEL),
        "ffn2_w_down": nrm(ks[21], (L, D_FF, D_MODEL), D_FF),
        "final_norm": gain(ks[22], (D_MODEL,)),
    }

def second_block(x, norm_ffn1, ffn1_w_up, ffn1_w_down, norm_mix, w_in, pool_w, pool_b, pool_scale,
              w_pool_up, conv_w, conv_b, lru_w_a, lru_b_a, lru_w_x, lru_b_x, lru_lambda, w_lru_up,
              w_out, norm_ffn2, ffn2_w_up, ffn2_w_down, final_norm):
    for l in range(DEPTH):
        x = x + 0.5 * swiglu_ffn(rmsnorm_2(x, norm_ffn1[l]), ffn1_w_up[l], ffn1_w_down[l])
        x = x + hybrid_mixer(rmsnorm_2(x, norm_mix[l]), w_in[l], pool_w[l], pool_b[l], pool_scale[l],
                             w_pool_up[l], conv_w[l], conv_b[l], lru_w_a[l], lru_b_a[l],
                             lru_w_x[l], lru_b_x[l], lru_lambda[l], w_lru_up[l], w_out[l])
        x = x + 0.5 * swiglu_ffn(rmsnorm_2(x, norm_ffn2[l]), ffn2_w_up[l], ffn2_w_down[l])
    return rmsnorm_2(x, final_norm)


def setup_inputs(seed=0):
    out = dict(first_inputs(seed))
    for name, value in second_inputs(seed + 1).items():
        if name != "x":
            out[name + "_2"] = value
    return out


def reference(
    x, c, ada_w, ada_b, norm_mix, norm_ffn, a_w_in, a_b_in, a_ln_g, a_ln_b, a_w_s, a_b_s,
    a_w_out, kv_norm, kv_ada_w, kv_ada_b, kv_w_k, kv_w_v, b_w_q, b_w_o, moe_router, moe_bias,
    moe_w_gate, moe_w_up, moe_w_down, sh_w_gate, sh_w_up, sh_w_down, final_norm, norm_ffn1_2,
    ffn1_w_up_2, ffn1_w_down_2, norm_mix_2, w_in_2, pool_w_2, pool_b_2, pool_scale_2,
    w_pool_up_2, conv_w_2, conv_b_2, lru_w_a_2, lru_b_a_2, lru_w_x_2, lru_b_x_2, lru_lambda_2,
    w_lru_up_2, w_out_2, norm_ffn2_2, ffn2_w_up_2, ffn2_w_down_2, final_norm_2,
):
    x = first_block(
        x, c, ada_w, ada_b, norm_mix, norm_ffn, a_w_in, a_b_in, a_ln_g, a_ln_b, a_w_s, a_b_s,
        a_w_out, kv_norm, kv_ada_w, kv_ada_b, kv_w_k, kv_w_v, b_w_q, b_w_o, moe_router,
        moe_bias, moe_w_gate, moe_w_up, moe_w_down, sh_w_gate, sh_w_up, sh_w_down, final_norm,
    )
    return second_block(
        x, norm_ffn1_2, ffn1_w_up_2, ffn1_w_down_2, norm_mix_2, w_in_2, pool_w_2, pool_b_2,
        pool_scale_2, w_pool_up_2, conv_w_2, conv_b_2, lru_w_a_2, lru_b_a_2, lru_w_x_2,
        lru_b_x_2, lru_lambda_2, w_lru_up_2, w_out_2, norm_ffn2_2, ffn2_w_up_2, ffn2_w_down_2,
        final_norm_2,
    )


_drawn_inputs = setup_inputs


def setup_inputs(seed=0):
    import zlib

    import numpy as np

    out = dict(_drawn_inputs(seed))
    spreads = {}
    factors = {'norm_mix': 8.0,
     'norm_ffn': 2.809,
     'a_b_in': 8.0,
     'a_ln_g': 8.0,
     'a_ln_b': 8.0,
     'a_b_s': 8.0,
     'kv_norm': 8.0,
     'kv_ada_b': 8.0,
     'norm_ffn1_2': 4.689,
     'norm_mix_2': 3.841,
     'pool_b_2': 54.765,
     'conv_b_2': 3.251,
     'lru_b_a_2': 48.228,
     'lru_b_x_2': 24.067,
     'norm_ffn2_2': 5.632,
     'final_norm_2': 8.777}
    for name, (base, spread) in spreads.items():
        noise = np.random.default_rng([zlib.crc32(name.encode()), seed]).standard_normal(out[name].shape)
        drawn = base * np.exp(spread * noise) if base else spread * noise
        out[name] = __import__('jax').numpy.asarray(drawn.astype(out[name].dtype))
    for name, factor in factors.items():
        out[name] = (out[name] * factor).astype(out[name].dtype)
    return out
```

```python
from contextlib import ExitStack

import concourse.bass as bass
from concourse import mybir

F32 = mybir.dt.float32
BF16 = mybir.dt.bfloat16
ALU = mybir.AluOpType
ACT = mybir.ActivationFunctionType
AX = mybir.AxisListType

P = 128
D = 1024
K = D // P
S = 256
TT = S // P
W = 256
E = 64
EG = 8
PICK_GROUPS = 4
ROUTED_SCALE = 2.5
CHUNK_GROUPS = 8
AW = 2048
HEADS = 16
DH = 64
FF_UNITS = 2816 // W
POOL_UNITS = 512 // W
LRU_UNITS = 1280 // W
LH = 10
CONV = 4
PADP = 8
PADC = CONV - 1
LAYERS = 2
UNIT = 2048
RING = 12
GROUPS_PER_TURN = 4
RMS_EPS = 1e-6
LN_EPS = 1e-5
NEG = -1e30
GONE = -3e38
TOP = 3e38

UPDATES = ["gm", "moe0", "at", "moe1", "fin", "ffn1_0", "mix_0", "ffn2_0", "ffn1_1", "mix_1", "ffn2_1"]
NORMS = ["in"] + UPDATES


class Books:

    def __init__(self):
        self.n = {}
        self.at = {}

    def book(self, what, key, count=1):
        self.at[what, key] = self.n.get(what, 0)
        self.n[what] = self.at[what, key] + count

    def own(self, bk, key, count=1):
        self.book(bk, key, count)
        self.book("own" + bk, key, count)

    def pair(self, key, count, own=True):
        book = self.own if own else self.book
        book("G", key, (count + 1) // 2)
        book("U", key, count // 2)


def book_all():
    b = Books()
    b.pair("x", 4)
    b.own("B", "norm_in")
    b.pair("ws", 2)
    b.book("unit", "ada_first", 8)
    b.book("unit", "gm", 3 * 24)
    b.book("M", "ada_first")
    b.book("M", "ada_rest")
    b.pair("gm_in", 16, own=False)
    b.pair("sv", CHUNK_GROUPS)
    for m in range(2):
        b.own("B", "norm_" + ("gm" if m == 0 else "at"))
        key = f"moe{m}"
        b.own("M", key + "scores")
        b.own("M", key + "weights")
        b.book("G", key, E + 1)
        b.book("U", key, E + 1)
        b.own("B", key, E)
        b.book("unit", key, 3 * (E + 1))
        if m == 0:
            b.own("B", "norm_moe0")
            b.book("unit", "at", 16)
            b.pair("qkv", 12, own=False)
            b.pair("heads", HEADS)
            b.own("B", "heads", HEADS)
            b.own("M", "heads", HEADS // 2)
    b.own("B", "norm_moe1")
    b.own("B", "norm_fin")
    for l in range(LAYERS):
        b.book("unit", f"ffn1_{l}", 3 * FF_UNITS)
        b.book("G", f"ffn1_{l}", FF_UNITS)
        b.book("U", f"ffn1_{l}", FF_UNITS)
        b.own("B", f"norm_ffn1_{l}")
        b.book("unit", f"mix_{l}", 12 + 8 + 2 + 5 + 4)
        b.pair(f"in_{l}", 12, own=False)
        b.pair(f"gates_{l}", LH)
        b.own("M", f"pool_{l}", 2)
        for part in ("gp", "gl", "yp", "yl"):
            b.book("Y", f"{part}_{l}")
        b.own("B", f"norm_mix_{l}")
        b.book("unit", f"ffn2_{l}", 3 * FF_UNITS)
        b.book("G", f"ffn2_{l}", FF_UNITS)
        b.book("U", f"ffn2_{l}", FF_UNITS)
        b.own("B", f"norm_ffn2_{l}")
    b.pair("final", 4)
    return b


def build(nc, A, out):
    b = book_all()
    with ExitStack() as ctx:
        def sb(name, shape, dt=F32):
            return ctx.enter_context(nc.sbuf_tensor(name, shape, dt))

        def sem(name):
            return ctx.enter_context(nc.semaphore(name))

        ring = sb("ring", [P, RING, UNIT])
        x = sb("x", [P, K, S])
        h = sb("h", [P, K, S])
        arena = sb("arena", [P, 17984])
        ident = sb("ident", [P, P])
        ones = sb("ones", [P, P])
        zero16 = sb("zero16", [P, 512], BF16)
        mask = sb("mask", [P, TT, S])
        rstd = sb("rstd", [P, S])
        silu = sb("silu", [P, 2, S])
        hidden = sb("hidden", [P, 2, 2, S])
        router = sb("router", [P, 2, K, E])
        rbias = sb("rbias", [P, 2, E])
        wt = sb("wt", [E, S])
        gate_row = sb("gate_row", [E, 2, S])
        cvec = sb("cvec", [P, K])
        cact = sb("cact", [P, K])
        adab = sb("adab", [P, 14 * K])
        ada = sb("ada", [P, 14 * K])
        gains = sb("gains", [P, 13, K])
        coef = sb("coef", [P, 5, K])
        bias_u = sb("bias_u", [P, CHUNK_GROUPS, 2])
        convw = sb("convw", [P, LAYERS, CONV, LH])
        convb = sb("convb", [P, LAYERS, LH])
        lam = sb("lam", [P, LAYERS, LH])
        ba = sb("ba", [P, LAYERS, LH])
        bx = sb("bx", [P, LAYERS, LH])
        poolb = sb("poolb", [P, LAYERS, 4])
        pools = sb("pools", [P, LAYERS, 4])
        sp = sb("sp", [P, 5, LAYERS, LH])
        inv_count = sb("inv_count", [P, 4, 16])
        stat = sb("stat", [P, 64])
        nmax = sb("nmax", [P, 2, 8])
        eps = sb("eps", [P, 2])

        bank = {
            "Y": ctx.enter_context(nc.psum_tensor("Y", [P, K, S], F32)),
            "G": ctx.enter_context(nc.psum_tensor("G", [P, 2, S], F32)),
            "U": ctx.enter_context(nc.psum_tensor("U", [P, 2, S], F32)),
            "B": ctx.enter_context(nc.psum_tensor("B", [P, 2, S], F32)),
            "M": ctx.enter_context(nc.psum_tensor("M", [P, 2, S], F32)),
        }
        Y = bank["Y"]

        def area(at, *dims):
            n = 1
            for d in dims:
                n *= d
            v = arena[:, at:at + n]
            names = "abcd"[:len(dims)]
            if len(dims) == 1:
                return v
            return v.rearrange(f"p ({' '.join(names)}) -> p {' '.join(names)}", **dict(zip(names, dims)))

        vtok = area(0, TT, AW)
        ut = area(4096, 2 * CHUNK_GROUPS, S)
        xtok = area(4096, TT, D)
        lng = area(8192, AW)
        lnb = area(10240, AW)
        ws = area(12288, CHUNK_GROUPS, P)
        wst = area(13312, CHUNK_GROUPS, P)
        bv_row = area(14336, AW)
        bs_row = area(16384, CHUNK_GROUPS * P)
        score = area(0, TT, E)
        choice = area(128, TT, E)
        taken = area(256, TT, E)
        wtok = area(384, TT, E)
        best8 = area(512, TT, EG, 8)
        grp12 = area(640, TT, 12)
        grp8 = area(664, TT, 8)
        grpt = area(680, TT, 12)
        gmask = area(704, TT, 8)
        goff = area(720, TT, 8)
        top8 = area(736, TT, 8)
        wsum = area(752, TT)
        qt_ = area(0, K, S)
        kt_ = area(2048, K, S)
        va = area(4096, TT, D)
        ot = area(6144, K, S)
        hkv = area(8192, K, S)
        smx = area(10240, 2, TT, S)
        prob = area(11264, 2, TT, S)
        pt = area(12288, 2, 384)
        u_lru = area(0, LH, PADC + S)
        vconv = area(2592, LH, S)
        gl = area(5152, LH, S)
        ra = area(7712, LH, S)
        ia = area(10272, LH, S)
        tl = arena[:, 0:LH * S].rearrange("p (a b) -> p a b", a=LH)
        pl0 = area(12832, 4, PADP + S)
        pl1 = area(7712, 4, PADP + S)
        pl2 = area(10272, 4, PADP + S)
        gpool = area(13888, K, S)
        glru = area(15936, K, S)
        wa = area(13888, LH, P)
        wx = area(15168, LH, P)
        poolw = sb("poolw", [P, 4, P])
        mixed = area(12832, 4, S)
        otok = area(0, TT, D)

        def pools_of(g):
            return (pl1 if g % 2 == 0 else pl2)[:, g, PADP:]

        landed = [sem(f"landed{i}") for i in range(RING)]
        done = [sem(f"done{i}") for i in range(RING)]
        filled = {n: sem("filled" + n) for n in "GUBM"}
        drained = {n: sem("drained" + n) for n in "YGUBM"}
        x_in = sem("x_in")
        c_in = sem("c_in")
        small_in = sem("small_in")
        gm_in = sem("gm_in")
        lru_in = sem("lru_in")
        out_done = sem("out_done")
        consts = sem("consts")
        pool_step = sem("pool_step")
        cact_ready = sem("cact_ready")
        x_ready = sem("x_ready")
        sq_ready = sem("sq_ready")
        h_ready = sem("h_ready")
        hkv_ready = sem("hkv_ready")
        gv_ready = sem("gv_ready")
        weights_ready = sem("weights_ready")
        row_ready = sem("row_ready")
        nmax_ready = sem("nmax_ready")
        exp_done = sem("exp_done")
        prob_ready = sem("prob_ready")
        pooled_ready = sem("pooled_ready")
        conv_ready = sem("conv_ready")
        decay_ready = sem("decay_ready")
        soft_a = sem("soft_a")
        soft_b = sem("soft_b")
        soft_c = sem("soft_c")
        lru_ready = sem("lru_ready")
        z_ready = sem("z_ready")
        act_step = sem("act_step")
        var_ready = sem("var_ready")
        std_ready = sem("std_ready")
        square_ready = sem("square_ready")
        root_ready = sem("root_ready")
        dve_step = sem("dve_step")

        block = ctx.enter_context(nc.Block())

        def pair_bank(f):
            return "GU"[f % 2]

        def slot_of(n):
            return n % RING, n // RING

        def wait_done(eng, n, turn=0):
            s, t = slot_of(n)
            eng.wait_ge(done[s], turn + (t + 1))

        def wait_full(eng, bk, key, i=0):
            eng.wait_ge(filled[bk], i + (b.at["own" + bk, key] + 1))

        def wait_pair_full(eng, key, f):
            wait_full(eng, pair_bank(f), key, f // 2)

        def wait_drained(eng, bk, key, i=0):
            eng.wait_ge(drained[bk], i + (b.at[bk, key] + 1))

        def wait_pair_drained(eng, key, f):
            wait_drained(eng, pair_bank(f), key, f // 2)

        def wait_free(eng, bk, key, i=0):
            n = i + b.at[bk, key]
            if not (isinstance(n, int) and n == 0):
                eng.wait_ge(drained[bk], n)

        def wait_pair_free(eng, key, f):
            wait_free(eng, pair_bank(f), key, f // 2)

        small_total = []

        def cols(w, at):
            return w.rearrange("(p k) n -> p k n", k=K)[:, :, at:at + W]

        def rows_k(w, q, at):
            return w.rearrange("(p k) n -> p k n", k=K)[:, 2 * q:2 * q + 2, at:at + D]

        def rows_pc(w, n):
            return w[n * W:(n + 1) * W, :].rearrange("(p c) m -> p c m", c=2)

        def rows_cp(w, n):
            return w[n * W:(n + 1) * W, :].rearrange("(c p) m -> p c m", c=2)

        ada_units = [(A["ada_w"][0], q, s * D) for s in range(6) for q in range(4)] + \
                    [(A["ada_w"][1], q, s * D) for s in range(6) for q in range(4)] + \
                    [(A["kv_ada_w"], q, s * D) for s in range(2) for q in range(4)]

        def view_a(slot):
            return ring[:, slot, :].rearrange("p (k n) -> p k n", k=K)

        def view_b(slot):
            return ring[:, slot, :].rearrange("p (c n) -> p c n", c=2)

        @block.sync
        def _(eng):
            state = [0]

            def load(src, wide, slot=None, turn=None):
                if slot is None:
                    slot, turn = slot_of(state[0])
                    state[0] += 1
                if not (isinstance(turn, int) and turn == 0):
                    eng.wait_ge(done[slot], turn)
                dst = view_a(slot) if wide == K else view_b(slot)
                eng.dma_start(dst, src).then_inc(landed[slot], 16)

            def swiglu(gate, up, down, groups, first):
                base = state[0]
                head = first
                turns = (groups - head) // GROUPS_PER_TURN
                for n in range(head):
                    load(gate(n), K), load(up(n), K), load(down(n), 2)
                at = state[0]
                if turns:
                    with eng.Fori(0, turns) as i:
                        for g in range(GROUPS_PER_TURN):
                            for m, (f, wide) in enumerate(((gate, K), (up, K), (down, 2))):
                                s, t = slot_of(at + 3 * g + m)
                                load(f(i * GROUPS_PER_TURN + (head + g)), wide, s, i + t)
                state[0] = at + turns * RING
                for n in range(head + turns * GROUPS_PER_TURN, groups):
                    load(gate(n), K), load(up(n), K), load(down(n), 2)
                assert state[0] == base + 3 * groups

            for n in range(8):
                w, q, at = ada_units[n]
                load(rows_k(w, q, at), 2)
            assert state[0] == b.at["unit", "gm"]
            win, wout = A["a_w_in"][0], A["a_w_out"][0]
            rest = iter(ada_units[8:])
            for n in range(24):
                if n < 8:
                    load(cols(win, AW + n * W), K)
                elif n < 16:
                    load(cols(win, (n - 8) * W), K)
                else:
                    load(rows_pc(wout, n - 16), 2)
                for _ in range(2):
                    w, q, at = next(rest)
                    load(rows_k(w, q, at), 2)
            for m in range(2):
                assert state[0] == b.at["unit", f"moe{m}"]
                load(cols(A["sh_w_gate"][m], 0), K)
                load(cols(A["sh_w_up"][m], 0), K)
                load(rows_pc(A["sh_w_down"][m], 0), 2)
                swiglu(lambda e: cols(A["moe_w_gate"][m, e], 0), lambda e: cols(A["moe_w_up"][m, e], 0),
                       lambda e: rows_pc(A["moe_w_down"][m, e], 0), E, 0)
                if m == 0:
                    assert state[0] == b.at["unit", "at"]
                    for w in (A["b_w_q"][0], A["kv_w_k"], A["kv_w_v"]):
                        for n in range(4):
                            load(cols(w, n * W), K)
                    for n in range(4):
                        load(rows_cp(A["b_w_o"][0], n), 2)
            for l in range(LAYERS):
                def ffn(up_w, down_w):
                    gv = up_w.rearrange("(p k) (g n) -> g p k n", k=K, n=W)
                    dv = down_w.rearrange("(g p c) m -> g p c m", p=P, c=2)
                    swiglu(lambda n: gv[n], lambda n: gv[n + FF_UNITS], lambda n: dv[n], FF_UNITS, 1)

                assert state[0] == b.at["unit", f"ffn1_{l}"]
                ffn(A["ffn1_w_up_2"][l], A["ffn1_w_down_2"][l])
                assert state[0] == b.at["unit", f"mix_{l}"]
                w = A["w_in_2"][l]
                for n in range(12):
                    load(cols(w, n * W), K)
                for n in range(8):
                    load(rows_k(w, n % 4, 12 * W + (n // 4) * D), 2)
                for n in range(POOL_UNITS):
                    load(rows_cp(A["w_pool_up_2"][l], n), 2)
                for n in range(LRU_UNITS):
                    load(rows_cp(A["w_lru_up_2"][l], n), 2)
                for n in range(4):
                    load(rows_k(A["w_out_2"][l], n, 0), 2)
                assert state[0] == b.at["unit", f"ffn2_{l}"]
                ffn(A["ffn2_w_up_2"][l], A["ffn2_w_down_2"][l])
            for f in range(4):
                wait_pair_drained(eng, "final", f)
            eng.dma_start(out[0].rearrange("(t p) d -> p t d", p=P), otok).then_inc(out_done, 16)
            eng.wait_ge(out_done, 16)

        @block.gpsimd
        def _(eng):
            eng.memset(ident[:], 0.0).then_inc(pool_step, 1)
            eng.memset(mask[:], 0.0).then_inc(pool_step, 1)
            eng.memset(ones[:], 1.0)
            eng.memset(zero16[:], 0.0)
            eng.memset(eps[:, 0:1], RMS_EPS)
            eng.memset(eps[:, 1:2], LN_EPS)
            for t in range(15):
                eng.memset(inv_count[:, :, t:t + 1], 1.0 / (t + 1))
            eng.wait_ge(pool_step, 2)
            eng.affine_select(out=mask[:], in_=mask[:], compare_op=ALU.is_ge, fill=NEG, base=0,
                              pattern=[[P, TT], [-1, S]], channel_multiplier=1)
            eng.affine_select(out=ident[:], in_=ident[:], compare_op=ALU.not_equal, fill=1.0, base=0,
                              pattern=[[-1, P]], channel_multiplier=1).then_inc(consts, 1)
            eng.wait_ge(gm_in, 16 * 5)
            eng.affine_select(out=ws, in_=ws, compare_op=ALU.is_ge, fill=0.0, base=0,
                              pattern=[[0, CHUNK_GROUPS], [-1, P]], channel_multiplier=1).then_inc(consts, 1)

        @block.scalar
        def _(eng):
            def norm_squares(n):
                for f in range(4):
                    if n == 0:
                        wait_pair_drained(eng, "x", f)
                    else:
                        eng.wait_ge(x_ready, 4 * (n - 1) + f + 1)
                    eng.activation(h[:, 2 * f:2 * f + 2, :], x[:, 2 * f:2 * f + 2, :], ACT.Square)\
                       .then_inc(sq_ready, 1)
                if n == 0:
                    eng.wait_ge(consts, 1)
                wait_full(eng, "B", "norm_" + NORMS[n])
                eng.activation(rstd[:], bank["B"][:, 0, :], ACT.Sqrt, bias=eps[:, 0:1], scale=1.0 / D)\
                   .then_inc(drained["B"], 1)

            def silu_group(key, n, turn=0):
                wait_done(eng, b.at["unit", key] + 3 * n, turn)
                eng.wait_ge(drained["U"], turn * GROUPS_PER_TURN + (b.at["U", key] + n))
                eng.activation(silu[:], bank["G"][:], ACT.Silu).then_inc(drained["G"], 1)

            def swiglu(key, groups):
                turns = (groups - 1) // GROUPS_PER_TURN
                silu_group(key, 0)
                with eng.Fori(0, turns) as i:
                    for g in range(GROUPS_PER_TURN):
                        silu_group(key, 1 + g, i)
                for n in range(1 + turns * GROUPS_PER_TURN, groups):
                    silu_group(key, n)

            xv = A["x"][0].rearrange("(t p) d -> p t d", p=P)
            eng.dma_start(xtok, xv).then_inc(x_in, 16)
            eng.dma_start(cvec[:], A["c"][0].rearrange("(p k) -> p k", k=K)).then_inc(c_in, 16)
            gm = [(ws, A["a_w_s"][0].rearrange("g t s -> t g s")),
                  (lng, A["a_ln_g"][0].partition_broadcast(P)),
                  (lnb, A["a_ln_b"][0].partition_broadcast(P)),
                  (bv_row[0:1, :], A["a_b_in"][0].rearrange("(a n) -> a n", a=2)[1:2, :]),
                  (bs_row[0:1, :], A["a_b_s"][0].rearrange("(a g) t -> a (g t)", a=1))]
            per_k = "(p k) -> p k"
            small = [(adab[:, 0:48].rearrange("p (s k) -> p s k", k=K),
                      A["ada_b"][0].rearrange("(s p k) -> p s k", k=K, p=P)),
                     (adab[:, 48:96].rearrange("p (s k) -> p s k", k=K),
                      A["ada_b"][1].rearrange("(s p k) -> p s k", k=K, p=P)),
                     (adab[:, 96:112].rearrange("p (s k) -> p s k", k=K),
                      A["kv_ada_b"].rearrange("(s p k) -> p s k", k=K, p=P)),
                     (gains[:, 4, :], A["kv_norm"].rearrange(per_k, k=K)),
                     (gains[:, 11, :], A["final_norm_2"].rearrange(per_k, k=K)),
                     (gains[:, 12, :], A["final_norm"].rearrange(per_k, k=K)),
                     (bias_u[:], A["a_b_in"][0].rearrange("(a n p c) -> a p n c", a=2, p=P, c=2)[0])]
            for at, name in ((0, "norm_mix"), (2, "norm_ffn"), (5, "norm_ffn1_2"), (7, "norm_mix_2"), (9, "norm_ffn2_2")):
                small.append((gains[:, at:at + 2, :], A[name].rearrange("l (p k) -> p l k", k=K)))
            for l in range(LAYERS):
                small += [(router[:, l], A["moe_router"][l].rearrange("(p k) e -> p k e", k=K)),
                          (rbias[:, l, :], A["moe_bias"][l].partition_broadcast(P)),
                          (convb[:, l, :], A["conv_b_2"][l].rearrange("(a p) -> p a", p=P)),
                          (lam[:, l, :], A["lru_lambda_2"][l].rearrange("(a p) -> p a", p=P)),
                          (ba[:, l, :], A["lru_b_a_2"][l].rearrange("a p -> p a")),
                          (bx[:, l, :], A["lru_b_x_2"][l].rearrange("a p -> p a")),
                          (poolb[:, l, :], A["pool_b_2"][l].rearrange("a p -> p a")),
                          (pools[:, l, :], A["pool_scale_2"][l].rearrange("(a p) -> p a", p=P))]
                small += [(convw[:, l, j, :], A["conv_w_2"][l, j].rearrange("(a p) -> p a", p=P)) for j in range(CONV)]
            for dst, src in small:
                eng.dma_start(dst, src, allow_slow_non_contiguous=True).then_inc(small_in, 16)
            for dst, src in gm:
                eng.dma_start(dst, src).then_inc(gm_in, 16)
            small_total.append(16 * len(small))
            eng.wait_ge(c_in, 16)
            eng.activation(cact[:], cvec[:], ACT.Silu).then_inc(cact_ready, 1)
            norm_squares(0)
            eng.wait_ge(soft_a, 1)
            eng.activation(sp[:, 1], sp[:, 0], ACT.Exp, scale=-1.0).then_inc(soft_b, 1)

            for f in range(16):
                bk = pair_bank(f)
                wait_done(eng, b.at["unit", "gm"] + 3 * f)
                if f == 9:
                    eng.wait_ge(var_ready, 1)
                    eng.activation(stat[:, 50:55:4], stat[:, 49:54:4], ACT.Sqrt, bias=eps[:, 1:2]).then_inc(std_ready, 1)
                if f < 8:
                    eng.activation(vtok[:, :, f * W:(f + 1) * W], bank[bk][:], ACT.Gelu_apprx_tanh)\
                       .then_inc(drained[bk], 1)
                else:
                    g = f - 8
                    if g == 0:
                        eng.wait_ge(small_in, small_total[0])
                    eng.activation(ut[:, 2 * g, :], bank[bk][:, 0, :], ACT.Gelu_apprx_tanh, bias=bias_u[:, g, 0:1])
                    eng.activation(ut[:, 2 * g + 1, :], bank[bk][:, 1, :], ACT.Gelu_apprx_tanh,
                                   bias=bias_u[:, g, 1:2]).then_inc(drained[bk], 1)

            for m in range(2):
                norm_squares(1 if m == 0 else 3)
                wait_full(eng, "M", f"moe{m}scores")
                eng.activation(score, bank["M"][:, 0, 0:TT * E].rearrange("p (t e) -> p t e", t=TT), ACT.Sigmoid)\
                   .then_inc(drained["M"], 1)
                swiglu(f"moe{m}", E + 1)
                if m == 0:
                    norm_squares(2)
                    for f in range(12):
                        bk = pair_bank(f)
                        wait_done(eng, b.at["unit", "at"] + f)
                        dst = (qt_, kt_)[f // 4][:, 2 * (f % 4):2 * (f % 4) + 2, :] if f < 8 \
                            else va[:, :, (f - 8) * W:(f - 7) * W]
                        eng.activation(dst, bank[bk][:], ACT.Copy).then_inc(drained[bk], 1)

                    def turned(hd):
                        wait_full(eng, "B", "heads", hd)
                        eng.activation(pt[:, hd % 2, :], bank["B"][:].rearrange("p a s -> p (a s)")[:, 0:384], ACT.Copy)\
                           .then_inc(drained["B"], 1)
                        if hd % 2:
                            wait_full(eng, "M", "heads", hd // 2)
                            eng.activation(ot[:, hd // 2, :], bank["M"][:, 0, :], ACT.Copy).then_inc(drained["M"], 1)

                    for hd in range(HEADS):
                        eng.wait_ge(nmax_ready, hd + 1)
                        eng.activation(prob[:, hd % 2, 0, 0:P], smx[:, hd % 2, 0, 0:P], ACT.Exp,
                                       bias=nmax[:, hd % 2, 2:3], accum_out=nmax[:, hd % 2, 4:5])
                        eng.activation(prob[:, hd % 2, 1, :], smx[:, hd % 2, 1, :], ACT.Exp,
                                       bias=nmax[:, hd % 2, 3:4], accum_out=nmax[:, hd % 2, 5:6]).then_inc(exp_done, 1)
                        if hd >= 1:
                            turned(hd - 1)
                    turned(HEADS - 1)

            norm_squares(4)
            for l in range(LAYERS):
                norm_squares(5 + 3 * l)
                eng.dma_start(wa, A["lru_w_a_2"][l].rearrange("a d e -> d a e")).then_inc(lru_in, 16)
                eng.dma_start(wx, A["lru_w_x_2"][l].rearrange("a d e -> d a e")).then_inc(lru_in, 16)
                eng.dma_start(poolw[:], A["pool_w_2"][l].rearrange("a d e -> d a e")).then_inc(lru_in, 16)
                swiglu(f"ffn1_{l}", FF_UNITS)
                norm_squares(6 + 3 * l)
                for f in range(12):
                    bk = pair_bank(f)
                    wait_done(eng, b.at["unit", f"mix_{l}"] + f)
                    if f < 2:
                        eng.activation(pl0[:, 2 * f:2 * f + 2, PADP:], bank[bk][:], ACT.Copy).then_inc(drained[bk], 1)
                    elif f < 7:
                        g = 2 * (f - 2)
                        eng.activation(u_lru[:, g:g + 2, PADC:], bank[bk][:], ACT.Copy).then_inc(drained[bk], 1)
                    else:
                        g = 2 * (f - 7)
                        eng.activation(gl[:, g:g + 2, :], bank[bk][:], ACT.Gelu_apprx_tanh).then_inc(drained[bk], 1)
                for hd in range(LH):
                    bk = pair_bank(hd)
                    wait_pair_full(eng, f"gates_{l}", hd)
                    eng.activation(ra[:, hd, :], bank[bk][:, 0, :], ACT.Sigmoid, bias=ba[:, l, hd:hd + 1])\
                       .then_inc(act_step, 1)
                    eng.activation(ia[:, hd, :], bank[bk][:, 1, :], ACT.Sigmoid, bias=bx[:, l, hd:hd + 1])\
                       .then_inc(drained[bk], 1)
                eng.wait_ge(act_step, LH * (2 * l + 1))
                eng.wait_ge(soft_c, 1)
                for hd in range(LH):
                    eng.activation(tl[:, hd, :], ra[:, hd, :], ACT.Tanh, scale=sp[:, 0, l, hd:hd + 1])\
                       .then_inc(act_step, 1)
                eng.wait_ge(act_step, LH * (2 * l + 2))
                for hd in range(LH):
                    last = eng.activation(ra[:, hd, :], ra[:, hd, :], ACT.Exp, scale=sp[:, 1, l, hd:hd + 1])
                last.then_inc(decay_ready, 1)
                eng.wait_ge(square_ready, l + 1)
                eng.activation(tl, tl, ACT.Sqrt).then_inc(root_ready, 1)
                for part, dst in enumerate((gpool, glru)):
                    wait_done(eng, b.at["unit", f"mix_{l}"] + 12 + 4 * part + 3)
                    for j in range(4):
                        last = eng.activation(dst[:, 2 * j:2 * j + 2, :], Y[:, 2 * j:2 * j + 2, :], ACT.Sigmoid)
                    last.then_inc(drained["Y"], 1)
                norm_squares(7 + 3 * l)
                swiglu(f"ffn2_{l}", FF_UNITS)
            norm_squares(11)

        @block.tensor
        def _(eng):
            mm = eng.matmul

            def wait_unit(n, turn=0):
                s, t = slot_of(n)
                eng.wait_ge(landed[s], turn * 16 + 16 * (t + 1))
                return s

            def up_matmuls(s, bk, src, stride2, ready=None):
                u = view_a(s)
                for c in range(2):
                    for k in range(K):
                        if ready is not None and c == 0:
                            eng.wait_ge(ready[0], ready[1] + k + 1)
                        w = u[:, k, c::2] if stride2 else u[:, k, c * P:(c + 1) * P]
                        last = mm(bank[bk][:, c, :], lhsT=w, rhs=src[:, k, :], start=(k == 0), stop=(k == K - 1))
                last.then_inc(done[s], 1)

            def rows_matmuls(s, bk, src, bias=None, ready=None):
                u = view_a(s)
                for t in range(TT):
                    if bias is not None:
                        mm(bank[bk][:, t, :], lhsT=ones[0:1, :], rhs=bias, start=True, stop=False)
                    for k in range(K):
                        if ready is not None and t == 0:
                            eng.wait_ge(ready[0], ready[1] + k + 1)
                        last = mm(bank[bk][:, t, :], lhsT=src[:, k, t * P:(t + 1) * P], rhs=u[:, k, :],
                                  start=(bias is None and k == 0), stop=(k == K - 1))
                last.then_inc(done[s], 1)

            def down_matmuls(s, rhs, first, end):
                u = view_b(s)
                for j in range(K):
                    for c in range(2):
                        last = mm(Y[:, j, :], lhsT=u[:, c, j::K], rhs=rhs(c), start=(first and c == 0 and j % 2 == 0),
                                  stop=(end and c == 1), skip_group_check=True)
                last.then_inc(done[s], 1)

            def norm_sum(n):
                key = "norm_" + NORMS[n]
                wait_free(eng, "B", key)
                for k in range(K):
                    if k % 2 == 0:
                        eng.wait_ge(sq_ready, 4 * n + k // 2 + 1)
                    last = mm(bank["B"][:, 0, :], lhsT=ones[:], rhs=h[:, k, :], start=(k == 0), stop=(k == K - 1))
                last.then_inc(filled["B"], 1)

            def swiglu(key, groups, expert0, ready, between=None):
                unit0 = b.at["unit", key]

                def up_part(n, turn=0, rdy=None):
                    for q, bk in enumerate("GU"):
                        s = wait_unit(unit0 + 3 * n + q, turn)
                        wait_free(eng, bk, key, turn * GROUPS_PER_TURN + n)
                        up_matmuls(s, bk, h, True, rdy if q == 0 else None)

                def gate_part(n, turn):
                    eng.wait_ge(row_ready, turn * GROUPS_PER_TURN + (expert0 + n))
                    wait_free(eng, "B", key, turn * GROUPS_PER_TURN + (n - 1))
                    mm(bank["B"][:, 0, :], lhsT=ones[0:E, :], rhs=gate_row[:, n % 2, :], start=True, stop=True)\
                        .then_inc(filled["B"], 1)

                def down_part(n, turn=0, end=False):
                    s = wait_unit(unit0 + 3 * n + 2, turn)
                    wait_drained(eng, "U", key, turn * GROUPS_PER_TURN + n)
                    if expert0 is not None:
                        wait_drained(eng, "B", key, turn * GROUPS_PER_TURN + (n - 1))
                    down_matmuls(s, lambda c: hidden[:, n % 2, c, :], False, end)

                for j in range(4):
                    mm(Y[:, 2 * j:2 * j + 2, :], lhsT=zero16[:, 0:P], rhs=zero16[:], start=True, stop=False,
                       skip_group_check=True)
                up_part(0, rdy=ready)
                if between:
                    between()
                turns = (groups - 1) // GROUPS_PER_TURN
                with eng.Fori(0, turns) as i:
                    for g in range(GROUPS_PER_TURN):
                        up_part(1 + g, i)
                        if expert0 is not None:
                            gate_part(1 + g, i)
                        down_part(g, i)
                for n in range(1 + turns * GROUPS_PER_TURN, groups):
                    up_part(n)
                    down_part(n - 1)
                down_part(groups - 1, end=True)

            eng.wait_ge(consts, 1)
            eng.wait_ge(x_in, 16)
            for f in range(4):
                bk = pair_bank(f)
                wait_pair_free(eng, "x", f)
                for j in range(4):
                    k, t = 2 * f + j // 2, j % 2
                    last = eng.transpose(bank[bk][:, j // 2, t * P:(t + 1) * P], xtok[:, t, k::K], ident[:])
                last.then_inc(filled[bk], 1)
            norm_sum(0)
            eng.wait_ge(consts, 2)
            for f in range(2):
                bk = pair_bank(f)
                wait_pair_free(eng, "ws", f)
                for j in range(4):
                    last = eng.transpose(bank[bk][:, j // 2, (j % 2) * P:(j % 2 + 1) * P], ws[:, 4 * f + j, :], ident[:])
                last.then_inc(filled[bk], 1)

            def ada_unit(n, unit):
                s = wait_unit(unit)
                u = view_b(s)
                q = n % 4
                for j in range(K):
                    col = (n // 4) * K + j
                    for c in range(2):
                        last = mm(bank["M"][:, 0, col:col + 1], lhsT=u[:, c, j::K], rhs=cact[:, 2 * q + c:2 * q + c + 1],
                                  start=(n in (0, 8) and j == 0 and c == 0), stop=(q == 3 and c == 1),
                                  skip_group_check=True)
                last.then_inc(done[s], 1)

            eng.wait_ge(cact_ready, 1)
            for n in range(8):
                ada_unit(n, b.at["unit", "ada_first"] + n)

            eng.wait_ge(gm_in, 16 * 5)

            def sv(g):
                bk = pair_bank(g)
                wait_pair_free(eng, "sv", g)
                for c in range(2):
                    for t in range(TT):
                        o = bank[bk][:, c, t * P:(t + 1) * P]
                        mm(o, lhsT=vtok[:, t, g * W + c:(g + 1) * W:2], rhs=wst[:, g, :], start=True, stop=False)
                        last = mm(o, lhsT=ones[0:1, :], rhs=bs_row[0:1, g * P:(g + 1) * P], start=False, stop=True)
                last.then_inc(filled[bk], 1)

            for n in range(24):
                unit = b.at["unit", "gm"] + 3 * n
                if n < 16:
                    s = wait_unit(unit)
                    wait_pair_free(eng, "gm_in", n)
                    if n < 8:
                        rows_matmuls(s, pair_bank(n), h, bv_row[0:1, n * W:(n + 1) * W], (h_ready, 0) if n == 0 else None)
                    else:
                        up_matmuls(s, pair_bank(n), h, True)
                else:
                    g = n - 16
                    if g == 0:
                        eng.wait_ge(gv_ready, 1)
                        sv(0)
                    if g + 1 < CHUNK_GROUPS:
                        sv(g + 1)
                    s = wait_unit(unit)
                    wait_pair_drained(eng, "sv", g)
                    down_matmuls(s, lambda c: ut[:, 2 * g + c, :], g == 0, g == 7)
                if n == 0:
                    wait_free(eng, "M", "ada_rest")
                for m in range(2):
                    ada_unit(8 + 2 * n + m, unit + 1 + m)

            for m in range(2):
                key = f"moe{m}"
                norm_sum(1 + 2 * m)
                hr = 8 * (1 + 2 * m)
                wait_free(eng, "M", key + "scores")
                if m == 0:
                    eng.wait_ge(small_in, small_total[0])
                for t in range(TT):
                    for k in range(K):
                        if t == 0:
                            eng.wait_ge(h_ready, hr + k + 1)
                        last = mm(bank["M"][:, 0, t * E:(t + 1) * E], lhsT=h[:, k, t * P:(t + 1) * P],
                                  rhs=router[:, m, k, :], start=(k == 0), stop=(k == K - 1))
                last.then_inc(filled["M"], 1)

                def turn_weights():
                    eng.wait_ge(weights_ready, m + 1)
                    wait_free(eng, "M", key + "weights")
                    for t in range(TT):
                        last = eng.transpose(bank["M"][0:E, 0, t * P:(t + 1) * P], wtok[:, t, :], ident[:])
                    last.then_inc(filled["M"], 1)

                swiglu(key, E + 1, E * m, None, turn_weights)
                if m == 1:
                    break
                norm_sum(2)
                at0 = b.at["unit", "at"]
                for f in range(12):
                    s = wait_unit(at0 + f)
                    wait_pair_free(eng, "qkv", f)
                    if f < 4:
                        up_matmuls(s, pair_bank(f), h, False, (h_ready, 16) if f == 0 else None)
                    elif f < 8:
                        up_matmuls(s, pair_bank(f), hkv, False, (hkv_ready, 0) if f == 4 else None)
                    else:
                        rows_matmuls(s, pair_bank(f), hkv)
                for f in range(12):
                    wait_pair_drained(eng, "qkv", f)

                def scores(hd):
                    bk, ch, p0 = pair_bank(hd), hd // 2, DH * (hd % 2)
                    wait_pair_free(eng, "heads", hd)
                    for t in range(TT):
                        last = mm(bank[bk][:, t, :], lhsT=qt_[p0:p0 + DH, ch, t * P:(t + 1) * P],
                                  rhs=kt_[p0:p0 + DH, ch, :], start=True, stop=True)
                    last.then_inc(filled[bk], 1)

                def values(hd):
                    ch, p0 = hd // 2, DH * (hd % 2)
                    eng.wait_ge(prob_ready, hd + 1)
                    wait_free(eng, "B", "heads", hd)
                    o = bank["B"][:].rearrange("p a s -> p (a s)")
                    pr = prob[:, hd % 2]
                    eng.transpose(o[:, 0:P], pr[:, 0, 0:P], ident[:])
                    eng.transpose(o[:, P:2 * P], pr[:, 1, 0:P], ident[:])
                    eng.transpose(o[:, 2 * P:3 * P], pr[:, 1, P:2 * P], ident[:]).then_inc(filled["B"], 1)
                    wait_drained(eng, "B", "heads", hd)
                    if hd % 2 == 0:
                        wait_free(eng, "M", "heads", hd // 2)
                    o = bank["M"][p0:p0 + DH, 0, :]
                    mm(o, lhsT=va[:, 0, hd * DH:(hd + 1) * DH], rhs=pt[:, hd % 2, 0:S], start=True, stop=False,
                       skip_group_check=True)
                    last = mm(o[:, P:S], lhsT=va[:, 1, hd * DH:(hd + 1) * DH], rhs=pt[:, hd % 2, S:S + P], start=False,
                              stop=True, skip_group_check=True)
                    if hd % 2:
                        last.then_inc(filled["M"], 1)

                scores(0)
                for hd in range(HEADS):
                    if hd + 1 < HEADS:
                        scores(hd + 1)
                    values(hd)
                for q in range(4):
                    s = wait_unit(at0 + 12 + q)
                    wait_drained(eng, "M", "heads", 2 * q + 1)
                    down_matmuls(s, lambda c: ot[:, 2 * q + c, :], q == 0, q == 3)

            norm_sum(4)
            for l in range(LAYERS):
                norm_sum(5 + 3 * l)
                swiglu(f"ffn1_{l}", FF_UNITS, None, (h_ready, 8 * (4 + 3 * l)))
                norm_sum(6 + 3 * l)
                unit = b.at["unit", f"mix_{l}"]
                for f in range(12):
                    s = wait_unit(unit + f)
                    wait_pair_free(eng, f"in_{l}", f)
                    up_matmuls(s, pair_bank(f), h, False, (h_ready, 8 * (5 + 3 * l)) if f == 0 else None)
                eng.wait_ge(lru_in, 48 * (l + 1))
                for f in range(2):
                    wait_free(eng, "M", f"pool_{l}", f)
                    eng.wait_ge(pooled_ready, l + 1)
                    for c in range(2):
                        g = 2 * f + c
                        last = mm(bank["M"][:, c, :], lhsT=poolw[:, g, :], rhs=pools_of(g), start=True, stop=True)
                    last.then_inc(filled["M"], 1)
                for hd in range(LH):
                    bk = pair_bank(hd)
                    eng.wait_ge(conv_ready, LH * l + hd + 1)
                    wait_pair_free(eng, f"gates_{l}", hd)
                    mm(bank[bk][:, 0, :], lhsT=wa[:, hd, :], rhs=vconv[:, hd, :], start=True, stop=True)
                    mm(bank[bk][:, 1, :], lhsT=wx[:, hd, :], rhs=vconv[:, hd, :], start=True, stop=True)\
                        .then_inc(filled[bk], 1)
                for part in range(2):
                    if part:
                        wait_drained(eng, "Y", f"gp_{l}")
                    for q in range(4):
                        s = wait_unit(unit + 12 + 4 * part + q)
                        down_matmuls(s, lambda c: h[:, 2 * q + c, :], q == 0, q == 3)
                wait_drained(eng, "Y", f"gl_{l}")
                wait_drained(eng, "M", f"pool_{l}", 1)
                for q in range(POOL_UNITS):
                    s = wait_unit(unit + 20 + q)
                    down_matmuls(s, lambda c: mixed[:, 2 * q + c, :], q == 0, q == POOL_UNITS - 1)
                wait_drained(eng, "Y", f"yp_{l}")
                eng.wait_ge(lru_ready, l + 1)
                for q in range(LRU_UNITS):
                    s = wait_unit(unit + 22 + q)
                    down_matmuls(s, lambda c: gl[:, 2 * q + c, :], q == 0, q == LRU_UNITS - 1)
                wait_drained(eng, "Y", f"yl_{l}")
                eng.wait_ge(z_ready, l + 1)
                for q in range(4):
                    s = wait_unit(unit + 27 + q)
                    down_matmuls(s, lambda c: gpool[:, 2 * q + c, :], q == 0, q == 3)
                norm_sum(7 + 3 * l)
                swiglu(f"ffn2_{l}", FF_UNITS, None, (h_ready, 8 * (6 + 3 * l)))
            norm_sum(11)
            eng.wait_ge(h_ready, 8 * 11)
            for f in range(4):
                bk, t = pair_bank(f), f // 2
                wait_pair_free(eng, "final", f)
                for j in range(4):
                    k = 4 * (f % 2) + j
                    last = eng.transpose(bank[bk][:, j // 2, (j % 2) * P:(j % 2 + 1) * P], h[:, k, t * P:(t + 1) * P],
                                         ident[:])
                last.then_inc(filled[bk], 1)

        @block.vector
        def _(eng):
            steps = [0]

            def link(ins):
                steps[0] += 1
                ins.then_inc(dve_step, 1)
                eng.wait_ge(dve_step, steps[0])

            def mark(ins):
                steps[0] += 1
                ins.then_inc(dve_step, 1)
                return steps[0]

            def norm(n, outs):
                key = "norm_" + NORMS[n]
                wait_drained(eng, "B", key)
                link(eng.reciprocal(rstd[:], rstd[:]))
                for dst, gain, shift, ready in outs:
                    scaled = []

                    def add_shift(k):
                        eng.wait_ge(dve_step, scaled[k])
                        eng.tensor_scalar(dst[:, k, :], dst[:, k, :], shift[:, k:k + 1], None, ALU.add).then_inc(ready, 1)

                    for k in range(K):
                        o = eng.scalar_tensor_tensor(out=dst[:, k, :], in0=x[:, k, :], scalar=gain[:, k:k + 1], in1=rstd[:],
                                                     op0=ALU.mult, op1=ALU.mult)
                        if shift is None:
                            if ready is not x_ready or k % 2:
                                o.then_inc(ready, 1)
                        else:
                            scaled.append(mark(o))
                            if k:
                                add_shift(k - 1)
                    if shift is not None:
                        add_shift(K - 1)
                if outs[0][3] is x_ready:
                    eng.wait_ge(x_ready, 4 * (n + 1))

            def update(u, last_unit, gain):
                wait_done(eng, last_unit)
                for j in range(4):
                    if isinstance(gain, float):
                        o = eng.scalar_tensor_tensor(out=x[:, 2 * j:2 * j + 2, :], in0=Y[:, 2 * j:2 * j + 2, :], scalar=gain,
                                                     in1=x[:, 2 * j:2 * j + 2, :], op0=ALU.mult, op1=ALU.add)
                    else:
                        for c in (2 * j, 2 * j + 1):
                            o = eng.scalar_tensor_tensor(out=x[:, c, :], in0=Y[:, c, :], scalar=gain[:, c:c + 1],
                                                         in1=x[:, c, :], op0=ALU.mult, op1=ALU.add)
                    o.then_inc(x_ready, 1)
                eng.wait_ge(x_ready, 4 * (u + 1))

            def hidden_group(key, n, expert=None, turn=0):
                unit0 = b.at["unit", key]
                i4 = turn * GROUPS_PER_TURN
                if expert is not None:
                    eng.tensor_scalar(gate_row[:, n % 2, :], wt[:], ident[0:E, bass.ds(expert, 1)], None, ALU.mult)\
                       .then_inc(row_ready, 1)
                wait_drained(eng, "G", key, i4 + n)
                wait_done(eng, unit0 + 3 * n + 1, turn)
                if n >= 1:
                    wait_done(eng, unit0 + 3 * (n - 2) + 2, turn)
                dst = hidden[:, n % 2]
                eng.tensor_tensor(dst, silu[:], bank["U"][:], ALU.mult).then_inc(drained["U"], 1)
                if expert is not None:
                    wait_drained(eng, "U", key, i4 + n)
                    wait_full(eng, "B", key, i4 + (n - 1))
                    eng.tensor_tensor(dst, dst, bank["B"][:, 0:1, :].broadcast_to([P, 2, S]), ALU.mult).then_inc(drained["B"], 1)

            def swiglu(key, groups, gated):
                turns = (groups - 1) // GROUPS_PER_TURN
                with eng.Fori(0, turns) as i:
                    for g in range(GROUPS_PER_TURN):
                        hidden_group(key, 1 + g, i * GROUPS_PER_TURN + g if gated else None, i)
                for n in range(1 + turns * GROUPS_PER_TURN, groups):
                    hidden_group(key, n)

            for f in range(4):
                bk = pair_bank(f)
                wait_pair_full(eng, "x", f)
                eng.tensor_copy(x[:, 2 * f:2 * f + 2, :], bank[bk][:]).then_inc(drained[bk], 1)
            eng.wait_ge(small_in, small_total[0])
            eng.scalar_tensor_tensor(out=sp[:, 0], in0=lam[:], scalar=-1.0, in1=lam[:], op0=ALU.mult, op1=ALU.max)\
               .then_inc(soft_a, 1)
            for f in range(2):
                bk = pair_bank(f)
                wait_pair_full(eng, "ws", f)
                eng.tensor_copy(wst[:, 4 * f:4 * f + 4, :], bank[bk][:].rearrange("p a (g s) -> p (a g) s", g=2))\
                   .then_inc(drained[bk], 1)
            eng.wait_ge(soft_b, 1)
            link(eng.tensor_scalar(sp[:, 2], sp[:, 1], 2.0, None, ALU.add))
            link(eng.reciprocal(sp[:, 2], sp[:, 2]))
            link(eng.tensor_tensor(sp[:, 2], sp[:, 2], sp[:, 1], ALU.mult))
            link(eng.tensor_tensor(sp[:, 3], sp[:, 2], sp[:, 2], ALU.mult))
            link(eng.tensor_scalar(sp[:, 4], sp[:, 3], 1.0 / 17, None, ALU.mult))
            for m in (15, 13, 11, 9, 7, 5, 3):
                link(eng.scalar_tensor_tensor(out=sp[:, 4], in0=sp[:, 4], scalar=1.0 / m, in1=sp[:, 3],
                                              op0=ALU.add, op1=ALU.mult))
            link(eng.scalar_tensor_tensor(out=sp[:, 4], in0=sp[:, 4], scalar=1.0, in1=sp[:, 2], op0=ALU.add, op1=ALU.mult))
            link(eng.tensor_scalar(sp[:, 3], lam[:], -1.0, 0.0, ALU.mult, ALU.max))
            link(eng.scalar_tensor_tensor(out=sp[:, 4], in0=sp[:, 4], scalar=2.0, in1=sp[:, 3], op0=ALU.mult, op1=ALU.add))
            eng.tensor_scalar(sp[:, 0], sp[:, 4], 8.0, None, ALU.mult)
            eng.tensor_scalar(sp[:, 1], sp[:, 4], -8.0, None, ALU.mult).then_inc(soft_c, 1)

            def vec(v):
                return ada[:, v * K:(v + 1) * K]

            def coefficient(at, gain, scale):
                link(eng.scalar_tensor_tensor(out=coef[:, at, :], in0=vec(scale), scalar=1.0, in1=gains[:, gain, :],
                                              op0=ALU.add, op1=ALU.mult))

            wait_done(eng, b.at["unit", "ada_first"] + 7)
            eng.tensor_tensor(ada[:, 0:16], bank["M"][:, 0, 0:16], adab[:, 0:16], ALU.add).then_inc(drained["M"], 1)
            wait_drained(eng, "M", "ada_first")
            coefficient(0, 0, 1)
            norm(0, [(h, coef[:, 0], vec(0), h_ready)])

            eng.wait_ge(gm_in, 16 * 5)
            for f in range(8):
                wait_pair_drained(eng, "gm_in", f)
            st = stat[:, 0:48].rearrange("p (t n s) -> p t n s", t=TT, n=4)
            for t in range(TT):
                for n in range(4):
                    s = mark(eng.bn_stats(st[:, t, n, :], vtok[:, t, n * 512:(n + 1) * 512]))
            eng.wait_ge(dve_step, s)
            for t in range(TT):
                o = eng.bn_aggr(stat[:, 48 + 4 * t:50 + 4 * t], st[:, t].rearrange("p n s -> p (n s)"))
            o.then_inc(var_ready, 1)
            eng.wait_ge(std_ready, 1)
            for t in range(TT):
                mv = stat[:, 48 + 4 * t:52 + 4 * t]
                link(eng.reciprocal(mv[:, 3:4], mv[:, 2:3]))
                link(eng.tensor_scalar(vtok[:, t, :], vtok[:, t, :], mv[:, 0:1], mv[:, 3:4], ALU.subtract, ALU.mult))
                link(eng.tensor_tensor(vtok[:, t, :], vtok[:, t, :], lng, ALU.mult))
                o = eng.tensor_tensor(vtok[:, t, :], vtok[:, t, :], lnb, ALU.add)
            o.then_inc(gv_ready, 1)
            for g in range(CHUNK_GROUPS):
                bk = pair_bank(g)
                wait_pair_drained(eng, "gm_in", 8 + g)
                wait_pair_full(eng, "sv", g)
                uu = ut[:, 2 * g:2 * g + 2, :]
                eng.tensor_tensor(uu, uu, bank[bk][:], ALU.mult).then_inc(drained[bk], 1)
            wait_done(eng, b.at["unit", "gm"] + 71)
            eng.tensor_tensor(ada[:, 16:112], bank["M"][:, 0, 16:112], adab[:, 16:112], ALU.add).then_inc(drained["M"], 1)
            wait_drained(eng, "M", "ada_rest")
            update(0, b.at["unit", "gm"] + 69, vec(2))
            coefficient(1, 2, 4)
            coefficient(2, 1, 7)
            coefficient(3, 3, 10)
            coefficient(4, 4, 13)

            for m in range(2):
                key = f"moe{m}"
                norm(1 + 2 * m, [(h, coef[:, 1 + 2 * m], vec(3 + 6 * m), h_ready)])
                link(eng.memset(grp12[:, :, 8:12], TOP))
                wait_drained(eng, "M", key + "scores")
                link(eng.tensor_tensor(choice, score, rbias[:, m:m + 1, :].broadcast_to([P, TT, E]), ALU.add))
                for t in range(TT):
                    for g in range(EG):
                        s = mark(eng.max(best8[:, t, g, :], choice[:, t, g * 8:(g + 1) * 8]))
                eng.wait_ge(dve_step, s)
                link(eng.tensor_tensor(grp12[:, :, 0:8], best8[:, :, :, 0], best8[:, :, :, 1], ALU.add))
                for t in range(TT):
                    link(eng.max(grp8[:, t, :], grp12[:, t, :]))
                    link(eng.match_replace(grpt[:, t, :], grp8[:, t, :], grp12[:, t, :], GONE))
                link(eng.tensor_scalar(gmask, grpt[:, :, 0:8], GONE, None, ALU.is_equal))
                link(eng.tensor_scalar(goff, gmask, -1.0, -NEG, ALU.add, ALU.mult))
                for t in range(TT):
                    cv = choice[:, t, :].rearrange("p (g e) -> p g e", g=EG)
                    link(eng.tensor_tensor(cv, cv, gmask[:, t, :].unsqueeze(2).broadcast_to([P, EG, 8]), ALU.mult))
                    link(eng.tensor_tensor(cv, cv, goff[:, t, :].unsqueeze(2).broadcast_to([P, EG, 8]), ALU.add))
                    link(eng.max(top8[:, t, :], choice[:, t, :]))
                    link(eng.match_replace(taken[:, t, :], top8[:, t, :], choice[:, t, :], GONE))
                link(eng.tensor_scalar(taken, taken, GONE, None, ALU.is_equal))
                link(eng.tensor_tensor(wtok, score, taken, ALU.mult))
                link(eng.tensor_reduce(wsum, wtok, AX.X, ALU.add))
                link(eng.reciprocal(wsum, wsum))
                for t in range(TT):
                    o = eng.tensor_scalar(wtok[:, t, :], wtok[:, t, :], wsum[:, t:t + 1], ROUTED_SCALE, ALU.mult, ALU.mult)
                o.then_inc(weights_ready, 1)
                hidden_group(key, 0)
                wait_full(eng, "M", key + "weights")
                eng.tensor_copy(wt[:], bank["M"][0:E, 0, :]).then_inc(drained["M"], 1)
                wait_drained(eng, "M", key + "weights")
                swiglu(key, E + 1, True)
                update(1 + 2 * m, b.at["unit", key] + 3 * E + 2, vec(5 + 6 * m))
                if m == 1:
                    break
                norm(2, [(h, coef[:, 2], vec(6), h_ready), (hkv, coef[:, 4], vec(12), hkv_ready)])

                def maxima(hd):
                    bk, q = pair_bank(hd), hd % 2
                    wait_pair_full(eng, "heads", hd)
                    eng.scalar_tensor_tensor(out=smx[:, q], in0=bank[bk][:], scalar=DH ** -0.5, in1=mask[:], op0=ALU.mult,
                                             op1=ALU.add).then_inc(drained[bk], 1)
                    wait_pair_drained(eng, "heads", hd)
                    link(eng.tensor_reduce(nmax[:, q, 0:2], smx[:, q], AX.X, ALU.max))
                    eng.tensor_scalar(nmax[:, q, 2:4], nmax[:, q, 0:2], -1.0, None, ALU.mult).then_inc(nmax_ready, 1)

                def normalise(hd):
                    q = hd % 2
                    eng.wait_ge(exp_done, hd + 1)
                    link(eng.reciprocal(nmax[:, q, 6:8], nmax[:, q, 4:6]))
                    eng.tensor_scalar(prob[:, q, 0, 0:P], prob[:, q, 0, 0:P], nmax[:, q, 6:7], None, ALU.mult)
                    eng.tensor_scalar(prob[:, q, 1, :], prob[:, q, 1, :], nmax[:, q, 7:8], None, ALU.mult)\
                       .then_inc(prob_ready, 1)

                maxima(0)
                for hd in range(HEADS):
                    if hd + 1 < HEADS:
                        maxima(hd + 1)
                    normalise(hd)
                update(2, b.at["unit", "at"] + 15, vec(8))

            norm(4, [(x, gains[:, 12], None, x_ready)])
            for l in range(LAYERS):
                norm(5 + 3 * l, [(h, gains[:, 5 + l], None, h_ready)])
                hidden_group(f"ffn1_{l}", 0)
                swiglu(f"ffn1_{l}", FF_UNITS, False)
                update(5 + 3 * l, b.at["unit", f"ffn1_{l}"] + 3 * FF_UNITS - 1, 0.5)
                norm(6 + 3 * l, [(h, gains[:, 7 + l], None, h_ready)])
                for buf in (pl0, pl1, pl2):
                    link(eng.memset(buf[:, :, 0:PADP], 0.0))
                link(eng.memset(u_lru[:, :, 0:PADC], 0.0))
                for f in range(2):
                    wait_pair_drained(eng, f"in_{l}", f)
                src = pl0
                for n in range(4):
                    dst = pl1 if n % 2 == 0 else pl2
                    w = 1 << n
                    link(eng.tensor_tensor(dst[:, n:4, PADP:], src[:, n:4, PADP:], src[:, n:4, PADP - w:PADP + S - w], ALU.add))
                    src = dst
                for g in range(4):
                    w = 2 << g
                    buf = pl1 if g % 2 == 0 else pl2
                    link(eng.tensor_tensor(buf[:, g, PADP:PADP + w - 1], buf[:, g, PADP:PADP + w - 1],
                                           inv_count[:, g, 0:w - 1], ALU.mult))
                    link(eng.tensor_scalar(buf[:, g, PADP + w - 1:], buf[:, g, PADP + w - 1:], 1.0 / w, None, ALU.mult))
                    o = eng.tensor_tensor(pools_of(g), pools_of(g), pl0[:, g, PADP:], ALU.subtract)
                o.then_inc(pooled_ready, 1)
                for hd in range(LH):
                    if hd % 2 == 0:
                        wait_pair_drained(eng, f"in_{l}", 2 + hd // 2)
                    v = vconv[:, hd, :]
                    link(eng.tensor_scalar(v, u_lru[:, hd, PADC:], convw[:, l, CONV - 1, hd:hd + 1], convb[:, l, hd:hd + 1],
                                           ALU.mult, ALU.add))
                    for j in range(CONV - 1):
                        o = eng.scalar_tensor_tensor(out=v, in0=u_lru[:, hd, j:j + S], scalar=convw[:, l, j, hd:hd + 1], in1=v,
                                                     op0=ALU.mult, op1=ALU.add)
                        if j < CONV - 2:
                            link(o)
                    o.then_inc(conv_ready, 1)
                for f in range(2):
                    wait_full(eng, "M", f"pool_{l}", f)
                    for c in range(2):
                        g = 2 * f + c
                        o = eng.tensor_scalar(mixed[:, g, :], bank["M"][:, c, :], poolb[:, l, g:g + 1], pools[:, l, g:g + 1],
                                              ALU.add, ALU.mult)
                    o.then_inc(drained["M"], 1)
                eng.wait_ge(decay_ready, l + 1)
                link(eng.tensor_tensor(ia, ia, vconv, ALU.mult))
                link(eng.tensor_scalar(vconv, tl, 1.0, None, ALU.add))
                link(eng.reciprocal(vconv, vconv))
                eng.scalar_tensor_tensor(out=tl, in0=tl, scalar=2.0, in1=vconv, op0=ALU.mult, op1=ALU.mult)\
                   .then_inc(square_ready, 1)
                eng.wait_ge(root_ready, l + 1)
                link(eng.tensor_tensor(ia, ia, tl, ALU.mult))
                for hd in range(LH):
                    s = mark(eng.tensor_tensor_scan(vconv[:, hd, :], ra[:, hd, :], ia[:, hd, :], 0.0, ALU.mult, ALU.add))
                eng.wait_ge(dve_step, s)
                for f in range(5):
                    wait_pair_drained(eng, f"in_{l}", 7 + f)
                eng.tensor_tensor(gl, gl, vconv, ALU.mult).then_inc(lru_ready, 1)
                wait_drained(eng, "Y", f"gl_{l}")
                for n, dst in enumerate((gpool, glru)):
                    wait_done(eng, b.at["unit", f"mix_{l}"] + (21, 26)[n])
                    for j in range(4):
                        o = eng.tensor_tensor(dst[:, 2 * j:2 * j + 2, :], dst[:, 2 * j:2 * j + 2, :],
                                              Y[:, 2 * j:2 * j + 2, :], ALU.mult)
                    o.then_inc(drained["Y"], 1)
                wait_drained(eng, "Y", f"yl_{l}")
                eng.tensor_tensor(gpool, gpool, glru, ALU.add).then_inc(z_ready, 1)
                update(6 + 3 * l, b.at["unit", f"mix_{l}"] + 30, 1.0)
                norm(7 + 3 * l, [(h, gains[:, 9 + l], None, h_ready)])
                hidden_group(f"ffn2_{l}", 0)
                swiglu(f"ffn2_{l}", FF_UNITS, False)
                update(7 + 3 * l, b.at["unit", f"ffn2_{l}"] + 3 * FF_UNITS - 1, 0.5)
            norm(11, [(h, gains[:, 11], None, h_ready)])
            for f in range(4):
                bk, t = pair_bank(f), f // 2
                wait_pair_full(eng, "final", f)
                dst = otok[:, t, :].rearrange("p (w k) -> p k w", k=K)[:, 4 * (f % 2):4 * (f % 2) + 4, :]
                eng.tensor_copy(dst, bank[bk][:].rearrange("p a (g w) -> p (a g) w", g=2)).then_inc(drained[bk], 1)


_INS = [
    'x', 'c', 'ada_w', 'ada_b', 'norm_mix', 'norm_ffn', 'a_w_in', 'a_b_in', 'a_ln_g', 'a_ln_b', 'a_w_s', 'a_b_s',
    'a_w_out', 'kv_norm', 'kv_ada_w', 'kv_ada_b', 'kv_w_k', 'kv_w_v', 'b_w_q', 'b_w_o', 'moe_router', 'moe_bias',
    'moe_w_gate', 'moe_w_up', 'moe_w_down', 'sh_w_gate', 'sh_w_up', 'sh_w_down', 'final_norm', 'norm_ffn1_2',
    'ffn1_w_up_2', 'ffn1_w_down_2', 'norm_mix_2', 'w_in_2', 'pool_w_2', 'pool_b_2', 'pool_scale_2',
    'w_pool_up_2', 'conv_w_2', 'conv_b_2', 'lru_w_a_2', 'lru_b_a_2', 'lru_w_x_2', 'lru_b_x_2', 'lru_lambda_2',
    'w_lru_up_2', 'w_out_2', 'norm_ffn2_2', 'ffn2_w_up_2', 'ffn2_w_down_2', 'final_norm_2',
]


def kernel(**inputs):
    import numpy as _np
    import concourse.bacc as _bacc
    from concourse import mybir as _mybir
    from concourse.bass_utils import run_bass_kernel_spmd as _run

    nc = _bacc.Bacc("TRN2", target_bir_lowering=False, num_devices=1)
    arrays, args = {}, {}
    for name in _INS:
        a = _np.ascontiguousarray(inputs[name])
        arrays[f"in_{name}_dram"] = a
        args[name] = nc.dram_tensor(f"in_{name}_dram", a.shape, _mybir.dt.from_np(a.dtype), kind="ExternalInput").ap()
    out = nc.dram_tensor("out_0_dram", (1, S, D), F32, kind="ExternalOutput").ap()
    build(nc, args, out)
    r = _run(nc, [arrays], core_ids=[0])
    return r.results[0]["out_0_dram"]
```

```python
from contextlib import ExitStack

import concourse.bass as bass
from concourse import mybir

F32 = mybir.dt.float32
F32R = mybir.dt.float32r
ALU = mybir.AluOpType
ACT = mybir.ActivationFunctionType
AX = mybir.AxisListType

P = 128
D = 1024
K = D // P
S = 256
TT = S // P
W = 256
E = 64
EG = 8
PICK_GROUPS = 4
ROUTED_SCALE = 2.5
CHUNK_GROUPS = 8
AW = 2048
HEADS = 16
DH = 64
FF_UNITS = 2816 // W
POOL_UNITS = 512 // W
LRU_UNITS = 1280 // W
LH = 10
CONV = 4
PADP = 8
PADC = CONV - 1
LAYERS = 2
UNIT = 2048
RING = 4
SPLIT = 3
GROUPS_PER_TURN = 4
PER_TURN = 3 * GROUPS_PER_TURN
ADA_FIRST = 8
ADA_MORE = 12
GM_UNITS = 24
FIRST = ADA_FIRST + ADA_MORE
VECTORS = [0, 1, 2, 3, 4, 5, 6, 7, 12, 13, 8, 9, 10, 11]
FILLS = {"ada_first": (0, 2), "ada_gm": (2, 3), "ada_ffn": (3, 5), "ada_moe": (5, 6), "ada_at": (6, 10),
         "ada_last": (10, 14)}
RMS_EPS = 1e-6
LN_EPS = 1e-5
NEG = -1e30
GONE = -3e38
TOP = 3e38

UPDATES = ["gm", "moe0", "at", "moe1", "fin", "ffn1_0", "mix_0", "ffn2_0", "ffn1_1", "mix_1", "ffn2_1"]
NORMS = ["in"] + UPDATES


class Books:

    def __init__(self):
        self.n = {}
        self.at = {}

    def book(self, what, key, count=1):
        self.at[what, key] = self.n.get(what, 0)
        self.n[what] = self.at[what, key] + count

    def own(self, bk, key, count=1):
        self.book(bk, key, count)
        self.book("own" + bk, key, count)

    def pair(self, key, count, own=True):
        book = self.own if own else self.book
        book("G", key, (count + 1) // 2)
        book("U", key, count // 2)

    def swiglu(self, key, groups):
        self.book("unit", key, 3 * groups)
        self.book("down", key, groups)
        self.book("G", key, groups)
        self.book("U", key, groups)


def book_all():
    b = Books()
    b.pair("x", 4)
    b.own("B", "norm_in")
    b.pair("ws", 2)
    b.book("unit", "gm", GM_UNITS)
    b.book("down", "gm", CHUNK_GROUPS)
    for key in ("ada_first", "ada_gm", "ada_ffn"):
        b.own("M", key)
    b.pair("gm_in", 16, own=False)
    b.pair("sv", CHUNK_GROUPS)
    for m in range(2):
        b.own("B", "norm_" + ("gm" if m == 0 else "at"))
        key = f"moe{m}"
        b.own("M", key + "scores")
        b.own("M", key + "weights")
        b.own("B", key, E)
        b.swiglu(key, E + 1)
        if m == 0:
            for fill in ("ada_moe", "ada_at", "ada_last"):
                b.own("M", fill)
            b.own("B", "norm_moe0")
            b.book("unit", "at", 16)
            b.book("down", "at", 4)
            b.pair("qkv", 12, own=False)
            b.pair("heads", HEADS)
            b.own("B", "heads", HEADS)
            b.own("M", "heads", HEADS // 2)
    b.own("B", "norm_moe1")
    b.own("B", "norm_fin")
    for l in range(LAYERS):
        b.swiglu(f"ffn1_{l}", FF_UNITS)
        b.own("B", f"norm_ffn1_{l}")
        b.book("unit", f"mix_{l}", 12 + 8 + 2 + 5 + 4)
        b.book("down", f"mix_{l}", 2 + 5 + 4)
        b.pair(f"in_{l}", 12, own=False)
        b.pair(f"gates_{l}", LH)
        b.own("M", f"pool_{l}", 2)
        for part in ("gp", "gl", "yp", "yl"):
            b.book("Y", f"{part}_{l}")
        b.own("B", f"norm_mix_{l}")
        b.swiglu(f"ffn2_{l}", FF_UNITS)
        b.own("B", f"norm_ffn2_{l}")
    b.pair("final", 4)
    return b


def swiglu_order(groups):
    order = [("gate", 0), ("up", 0)]
    for n in range(1, groups):
        order += [("gate", n), ("up", n), ("down", n - 1)]
    return order + [("down", groups - 1)]


def arrivals():
    order = [("ada", n) for n in range(ADA_FIRST)]
    for n in range(GM_UNITS):
        order += [("unit", n)]
        if n % 2 == 0:
            order += [("ada", ADA_FIRST + n // 2)]
    return order


def build(nc, A, out):
    b = book_all()
    with ExitStack() as ctx:
        def sb(name, shape, dt=F32):
            return ctx.enter_context(nc.sbuf_tensor(name, shape, dt))

        def sem(name):
            return ctx.enter_context(nc.semaphore(name))

        ring = sb("ring", [P, RING, UNIT])
        part_hi = sb("part_hi", [P, SPLIT, UNIT], F32R)
        part_lo = sb("part_lo", [P, SPLIT, UNIT], F32R)
        h_hi = sb("h_hi", [P, K, S], F32R)
        h_lo = sb("h_lo", [P, K, S], F32R)
        rows_hi = sb("rows_hi", [P, 2, 2, S], F32R)
        rows_lo = sb("rows_lo", [P, 2, 2, S], F32R)
        x = sb("x", [P, K, S])
        h = sb("h", [P, K, S])
        arena = sb("arena", [P, 16448])
        ident = sb("ident", [P, P])
        ones = sb("ones", [P, P])
        mask = sb("mask", [P, TT, S])
        rstd = sb("rstd", [P, S])
        swi = sb("swi", [P, 4, S])
        silu, hidden = swi[:, 0:2, :], swi[:, 2:4, :]
        router = sb("router", [P, 2, K, E])
        rbias = sb("rbias", [P, 2, E])
        wt = sb("wt", [E, S])
        gate_row = sb("gate_row", [E, 2, S])
        cvec = sb("cvec", [P, K])
        cact = sb("cact", [P, K])
        adab = sb("adab", [P, 14 * K])
        ada = sb("ada", [P, 14 * K])
        gains = sb("gains", [P, 13, K])
        coef = sb("coef", [P, 5, K])
        bias_u = sb("bias_u", [P, CHUNK_GROUPS, 2])
        convw = sb("convw", [P, LAYERS, CONV, LH])
        convb = sb("convb", [P, LAYERS, LH])
        lam = sb("lam", [P, LAYERS, LH])
        ba = sb("ba", [P, LAYERS, LH])
        bx = sb("bx", [P, LAYERS, LH])
        poolb = sb("poolb", [P, LAYERS, 4])
        pools = sb("pools", [P, LAYERS, 4])
        sp = sb("sp", [P, 5, LAYERS, LH])
        inv_count = sb("inv_count", [P, 4, 16])
        stat = sb("stat", [P, 64])
        nmax = sb("nmax", [P, 2, 8])
        eps = sb("eps", [P, 2])

        bank = {
            "Y": ctx.enter_context(nc.psum_tensor("Y", [P, K, S], F32)),
            "G": ctx.enter_context(nc.psum_tensor("G", [P, 2, S], F32)),
            "U": ctx.enter_context(nc.psum_tensor("U", [P, 2, S], F32)),
            "B": ctx.enter_context(nc.psum_tensor("B", [P, 2, S], F32)),
            "M": ctx.enter_context(nc.psum_tensor("M", [P, 2, S], F32)),
        }
        Y = bank["Y"]

        def area(at, *dims):
            n = 1
            for d in dims:
                n *= d
            v = arena[:, at:at + n]
            names = "abcd"[:len(dims)]
            if len(dims) == 1:
                return v
            return v.rearrange(f"p ({' '.join(names)}) -> p {' '.join(names)}", **dict(zip(names, dims)))

        vtok = area(0, TT, AW)
        ut = area(4096, 2 * CHUNK_GROUPS, S)
        xtok = area(4096, TT, D)
        lng = area(8192, AW)
        lnb = area(10240, AW)
        ws = area(12288, CHUNK_GROUPS, P)
        wst = area(13312, CHUNK_GROUPS, P)
        bv_row = area(6144, AW)
        bs_row = area(14336, CHUNK_GROUPS * P)
        late_ring = area(1024, 2, UNIT)

        def share(i):
            if i in (1, 3):
                return swi[:].rearrange("p a s -> p (a s)")
            return area({0: 15360, 2: 15360, 4: 12288, 10: 13312, 11: 14336, 12: 15360, 13: 10240}.get(i)
                        or 5120 + (i - 5) * D, D)

        score = area(0, TT, E)
        choice = area(128, TT, E)
        taken = area(256, TT, E)
        wtok = area(384, TT, E)
        best8 = area(512, TT, EG, 8)
        grp12 = area(640, TT, 12)
        grp8 = area(664, TT, 8)
        grpt = area(680, TT, 12)
        gmask = area(704, TT, 8)
        goff = area(720, TT, 8)
        top8 = area(736, TT, 8)
        wsum = area(752, TT)
        qt_ = area(0, K, S)
        kt_ = area(2048, K, S)
        va = area(4096, TT, D)
        ot = area(6144, K, S)
        hkv = area(8192, K, S)
        smx = area(10240, 2, TT, S)
        prob = area(11264, 2, TT, S)
        pt = area(12288, 2, 384)
        u_lru = area(0, LH, PADC + S)
        vconv = area(2592, LH, S)
        gl = area(5152, LH, S)
        ra = area(7712, LH, S)
        ia = area(10272, LH, S)
        tl = arena[:, 0:LH * S].rearrange("p (a b) -> p a b", a=LH)
        pl0 = area(12832, 4, PADP + S)
        pl1 = area(7712, 4, PADP + S)
        pl2 = area(10272, 4, PADP + S)
        gpool = h
        glru = area(13888, K, S)
        wa = area(13888, LH, P)
        wx = area(15168, LH, P)
        poolw = sb("poolw", [P, 4, P])
        mixed = area(12832, 4, S)
        otok = area(0, TT, D)

        def pools_of(g):
            return (pl1 if g % 2 == 0 else pl2)[:, g, PADP:]

        landed = [sem(f"landed{i}") for i in range(RING)]
        hi_ready = sem("hi_ready")
        lo_ready = sem("lo_ready")
        unit_done = sem("unit_done")
        ada_step = sem("ada_step")
        late_step = sem("late_step")
        ada_ready = sem("ada_ready")
        late_in = [sem(f"late_in{i}") for i in range(2)]
        rows_round = sem("rows_round")
        rows_ready = sem("rows_ready")
        raw_ready = sem("raw_ready")
        h_round = sem("h_round")
        filled = {n: sem("filled" + n) for n in "GUBM"}
        drained = {n: sem("drained" + n) for n in "YGUBM"}
        x_in = sem("x_in")
        c_in = sem("c_in")
        small_in = sem("small_in")
        gm_in = sem("gm_in")
        ln_in = sem("ln_in")
        lru_in = sem("lru_in")
        out_done = sem("out_done")
        consts = sem("consts")
        pool_step = sem("pool_step")
        cact_ready = sem("cact_ready")
        x_ready = sem("x_ready")
        sq_ready = sem("sq_ready")
        h_ready = sem("h_ready")
        gv_ready = sem("gv_ready")
        weights_ready = sem("weights_ready")
        row_ready = sem("row_ready")
        nmax_ready = sem("nmax_ready")
        exp_done = sem("exp_done")
        prob_ready = sem("prob_ready")
        pooled_ready = sem("pooled_ready")
        conv_ready = sem("conv_ready")
        decay_ready = sem("decay_ready")
        soft_a = sem("soft_a")
        soft_b = sem("soft_b")
        soft_c = sem("soft_c")
        act_step = sem("act_step")
        var_ready = sem("var_ready")
        std_ready = sem("std_ready")
        square_ready = sem("square_ready")
        root_ready = sem("root_ready")
        dve_step = sem("dve_step")

        block = ctx.enter_context(nc.Block())

        def pair_bank(f):
            return "GU"[f % 2]

        order = arrivals()

        def arrival(n, turn=0):
            at = order.index(("unit", n)) if n < GM_UNITS else n + FIRST
            return at % RING, turn * (16 * PER_TURN // RING) + 16 * (at // RING + 1)

        def wait_done(eng, n, turn=0):
            eng.wait_ge(unit_done, turn * PER_TURN + (n + 1))

        def wait_full(eng, bk, key, i=0):
            eng.wait_ge(filled[bk], i + (b.at["own" + bk, key] + 1))

        def wait_pair_full(eng, key, f):
            wait_full(eng, pair_bank(f), key, f // 2)

        def wait_drained(eng, bk, key, i=0):
            eng.wait_ge(drained[bk], i + (b.at[bk, key] + 1))

        def wait_pair_drained(eng, key, f):
            wait_drained(eng, pair_bank(f), key, f // 2)

        def wait_free(eng, bk, key, i=0):
            n = i + b.at[bk, key]
            if not (isinstance(n, int) and n == 0):
                eng.wait_ge(drained[bk], n)

        def wait_pair_free(eng, key, f):
            wait_free(eng, pair_bank(f), key, f // 2)

        small_total = []

        def cols(w, at):
            return w.rearrange("(p k) n -> p k n", k=K)[:, :, at:at + W]

        def rows_k(w, q, at):
            return w.rearrange("(p k) n -> p k n", k=K)[:, 2 * q:2 * q + 2, at:at + D]

        def rows_pc(w, n):
            return w[n * W:(n + 1) * W, :].rearrange("(p c) m -> p c m", c=2)

        def rows_cp(w, n):
            return w[n * W:(n + 1) * W, :].rearrange("(c p) m -> p c m", c=2)

        ada_units = [((A["ada_w"][v // 6] if v < 12 else A["kv_ada_w"]), q, (v % 6) * D) for v in VECTORS for q in range(4)]

        def view_a(unit):
            return unit.rearrange("p (k n) -> p k n", k=K)

        def view_b(unit):
            return unit.rearrange("p (c n) -> p c n", c=2)

        @block.sync
        def _(eng):
            state = [0]

            def wait_read(kind, n):
                if kind == "unit":
                    eng.wait_ge(lo_ready, n + 1)
                elif n % 4 == 3:
                    eng.wait_ge(ada_ready, n // 4 + 1)
                else:
                    eng.wait_ge(ada_step, 7 * (n // 4) + 2 * (n % 4) + 2)

            def load_ada(n):
                at = order.index(("ada", n))
                wait_slot(at)
                w, q, col = ada_units[n]
                eng.dma_start(view_b(ring[:, at % RING, :]), rows_k(w, q, col)).then_inc(landed[at % RING], 16)

            def wait_slot(at):
                if at >= RING:
                    kind, n = order[at - RING]
                    wait_read(kind, n)

            def load(src, wide, n=None, turn=0):
                if n is None:
                    n = state[0]
                    state[0] += 1
                if n < GM_UNITS:
                    wait_slot(order.index(("unit", n)))
                elif n < GM_UNITS + RING:
                    wait_slot_of_first(n)
                else:
                    eng.wait_ge(lo_ready, turn * PER_TURN + (n - RING + 1))
                slot, _ = arrival(n)
                dst = ring[:, slot, :]
                eng.dma_start(view_a(dst) if wide == K else view_b(dst), src).then_inc(landed[slot], 16)

            def wait_slot_of_first(n):
                kind, m = (order + [("unit", GM_UNITS + j) for j in range(RING)])[n + FIRST - RING]
                wait_read(kind, m)

            def swiglu(groups, gate, up, down, gate0=None, up0=None, down0=None):
                part = {"gate": (gate, K), "up": (up, K), "down": (down, 2)}
                first = {"gate": gate0 or gate, "up": up0 or up, "down": down0 or down}
                turns = (groups - 2) // GROUPS_PER_TURN
                seq = swiglu_order(groups)
                for p, n in seq[:5]:
                    load((first[p] if n == 0 else part[p][0])(n), part[p][1])
                at = state[0]
                with eng.Fori(0, turns) as i:
                    for j, (p, n) in enumerate(seq[5:5 + PER_TURN]):
                        load(part[p][0](i * GROUPS_PER_TURN + n), part[p][1], at + j, i)
                state[0] = at + turns * PER_TURN
                for p, n in seq[5 + turns * PER_TURN:]:
                    load(part[p][0](n), part[p][1])

            for n in range(ADA_FIRST):
                load_ada(n)
            win, wout = A["a_w_in"][0], A["a_w_out"][0]
            for n in range(GM_UNITS):
                if n < 8:
                    load(cols(win, AW + n * W), K)
                elif n < 16:
                    load(cols(win, (n - 8) * W), K)
                else:
                    load(rows_pc(wout, n - 16), 2)
                if n % 2 == 0:
                    load_ada(ADA_FIRST + n // 2)
            for m in range(2):
                assert state[0] == b.at["unit", f"moe{m}"]
                swiglu(E + 1, lambda n: cols(A["moe_w_gate"][m, n - 1], 0), lambda n: cols(A["moe_w_up"][m, n - 1], 0),
                       lambda n: rows_pc(A["moe_w_down"][m, n - 1], 0), lambda n: cols(A["sh_w_gate"][m], 0),
                       lambda n: cols(A["sh_w_up"][m], 0), lambda n: rows_pc(A["sh_w_down"][m], 0))
                if m == 0:
                    assert state[0] == b.at["unit", "at"]
                    for w in (A["b_w_q"][0], A["kv_w_k"], A["kv_w_v"]):
                        for n in range(4):
                            load(cols(w, n * W), K)
                    for n in range(4):
                        load(rows_cp(A["b_w_o"][0], n), 2)
            for l in range(LAYERS):
                def ffn(up_w, down_w):
                    gv = up_w.rearrange("(p k) (g n) -> g p k n", k=K, n=W)
                    dv = down_w.rearrange("(g p c) m -> g p c m", p=P, c=2)
                    swiglu(FF_UNITS, lambda n: gv[n], lambda n: gv[n + FF_UNITS], lambda n: dv[n])

                assert state[0] == b.at["unit", f"ffn1_{l}"]
                ffn(A["ffn1_w_up_2"][l], A["ffn1_w_down_2"][l])
                assert state[0] == b.at["unit", f"mix_{l}"]
                w = A["w_in_2"][l]
                for n in range(12):
                    load(cols(w, n * W), K)
                for n in range(8):
                    load(rows_k(w, n % 4, 12 * W + (n // 4) * D), 2)
                for n in range(POOL_UNITS):
                    load(rows_cp(A["w_pool_up_2"][l], n), 2)
                for n in range(LRU_UNITS):
                    load(rows_cp(A["w_lru_up_2"][l], n), 2)
                for n in range(4):
                    load(rows_k(A["w_out_2"][l], n, 0), 2)
                assert state[0] == b.at["unit", f"ffn2_{l}"]
                ffn(A["ffn2_w_up_2"][l], A["ffn2_w_down_2"][l])
            assert state[0] == b.n["unit"]
            for f in range(4):
                wait_pair_drained(eng, "final", f)
            eng.dma_start(out[0].rearrange("(t p) d -> p t d", p=P), otok).then_inc(out_done, 16)
            eng.wait_ge(out_done, 16)

        @block.gpsimd
        def _(eng):
            eng.memset(ident[:], 0.0).then_inc(pool_step, 1)
            eng.memset(mask[:], 0.0).then_inc(pool_step, 1)
            eng.memset(ones[:], 1.0)
            eng.memset(eps[:, 0:1], RMS_EPS)
            eng.memset(eps[:, 1:2], LN_EPS)
            for t in range(15):
                eng.memset(inv_count[:, :, t:t + 1], 1.0 / (t + 1))
            eng.wait_ge(pool_step, 2)
            eng.affine_select(out=mask[:], in_=mask[:], compare_op=ALU.is_ge, fill=NEG, base=0,
                              pattern=[[P, TT], [-1, S]], channel_multiplier=1)
            eng.affine_select(out=ident[:], in_=ident[:], compare_op=ALU.not_equal, fill=1.0, base=0,
                              pattern=[[-1, P]], channel_multiplier=1).then_inc(consts, 1)

            eng.wait_ge(gm_in, 16 * 3)
            eng.affine_select(out=ws, in_=ws, compare_op=ALU.is_ge, fill=0.0, base=0,
                              pattern=[[0, CHUNK_GROUPS], [-1, P]], channel_multiplier=1).then_inc(consts, 1)
            steps = [0]

            def step(o):
                o.then_inc(late_step, 1)
                steps[0] += 1

            def late(n):
                eng.wait_ge(late_in[n % 2], 16 * ((n - FIRST) // 2 + 1))
                dst, q = share(n // 4), n % 4
                u = view_b(late_ring[:, n % 2, :])
                parts = [dst if q == 0 else u[:, 0, :], u[:, 1, :]]
                for c in range(2):
                    step(eng.tensor_scalar(parts[c], u[:, c, :], cact[:, 2 * q + c:2 * q + c + 1], None, ALU.mult))
                for c in range(q == 0, 2):
                    eng.wait_ge(late_step, steps[0])
                    o = eng.tensor_tensor(dst, dst, parts[c], ALU.add)
                    if c == 1 and q == 3:
                        o.then_inc(ada_ready, 1)
                    else:
                        step(o)

            def load_late(n):
                w, q, col = ada_units[n]
                eng.dma_start(view_b(late_ring[:, n % 2, :]), rows_k(w, q, col)).then_inc(late_in[n % 2], 16)

            wait_done(eng, GM_UNITS - 1)
            wait_full(eng, "M", "ada_ffn")
            eng.wait_ge(cact_ready, 1)
            load_late(FIRST)
            load_late(FIRST + 1)
            for n in range(FIRST, len(ada_units)):
                late(n)
                if n + 2 < len(ada_units):
                    if n % 4 == 3:
                        eng.wait_ge(ada_ready, (n + 1) // 4)
                    else:
                        eng.wait_ge(late_step, steps[0])
                    load_late(n + 2)

        @block.scalar
        def _(eng):
            rounded = [0]

            def next_hi(count=1, turn=0):
                for _ in range(count):
                    n = rounded[0]
                    rounded[0] += 1
                    if n >= b.n["unit"]:
                        continue
                    slot, landing = arrival(n, turn)
                    eng.wait_ge(landed[slot], landing)
                    if n >= SPLIT:
                        eng.wait_ge(unit_done, turn * PER_TURN + (n - SPLIT + 1))
                    eng.activation(part_hi[:, n % SPLIT, :], ring[:, slot, :], ACT.Copy).then_inc(hi_ready, 1)

            raws = [0]

            def round_h(src, after=None):
                if after is not None:
                    wait_done(eng, after)
                for k in range(K):
                    eng.wait_ge(raw_ready, raws[0] + k + 1)
                    eng.activation(h_hi[:, k, :], src[:, k, :], ACT.Copy).then_inc(h_round, 1)
                raws[0] += K

            def norm_squares(n):
                for f in range(4):
                    if n == 0:
                        wait_pair_drained(eng, "x", f)
                    else:
                        eng.wait_ge(x_ready, 4 * (n - 1) + f + 1)
                    eng.activation(h[:, 2 * f:2 * f + 2, :], x[:, 2 * f:2 * f + 2, :], ACT.Square)\
                       .then_inc(sq_ready, 1)
                if n == 0:
                    eng.wait_ge(consts, 1)
                wait_full(eng, "B", "norm_" + NORMS[n])
                eng.activation(rstd[:], bank["B"][:, 0, :], ACT.Sqrt, bias=eps[:, 0:1], scale=1.0 / D)\
                   .then_inc(drained["B"], 1)

            def silu_group(key, n, turn=0):
                wait_done(eng, b.at["unit", key] + max(3 * n - 1, 0), turn)
                eng.wait_ge(drained["U"], turn * GROUPS_PER_TURN + (b.at["U", key] + n))
                eng.activation(silu, bank["G"][:], ACT.Silu).then_inc(drained["G"], 1)
                next_hi(2 if n == 0 else 3, turn)

            def swiglu(key, groups):
                turns = (groups - 2) // GROUPS_PER_TURN
                silu_group(key, 0)
                silu_group(key, 1)
                with eng.Fori(0, turns) as i:
                    for g in range(GROUPS_PER_TURN):
                        silu_group(key, 2 + g, i)
                rounded[0] += (turns - 1) * PER_TURN
                for n in range(2 + turns * GROUPS_PER_TURN, groups):
                    silu_group(key, n)

            xv = A["x"][0].rearrange("(t p) d -> p t d", p=P)
            eng.dma_start(xtok, xv).then_inc(x_in, 16)
            eng.dma_start(cvec[:], A["c"][0].rearrange("(p k) -> p k", k=K)).then_inc(c_in, 16)
            gm = [(ws, A["a_w_s"][0].rearrange("g t s -> t g s")),
                  (bv_row[0:1, :], A["a_b_in"][0].rearrange("(a n) -> a n", a=2)[1:2, :]),
                  (bs_row[0:1, :], A["a_b_s"][0].rearrange("(a g) t -> a (g t)", a=1))]
            per_k = "(p k) -> p k"
            small = [(adab[:, 0:48].rearrange("p (s k) -> p s k", k=K),
                      A["ada_b"][0].rearrange("(s p k) -> p s k", k=K, p=P)),
                     (adab[:, 48:96].rearrange("p (s k) -> p s k", k=K),
                      A["ada_b"][1].rearrange("(s p k) -> p s k", k=K, p=P)),
                     (adab[:, 96:112].rearrange("p (s k) -> p s k", k=K),
                      A["kv_ada_b"].rearrange("(s p k) -> p s k", k=K, p=P)),
                     (gains[:, 4, :], A["kv_norm"].rearrange(per_k, k=K)),
                     (gains[:, 11, :], A["final_norm_2"].rearrange(per_k, k=K)),
                     (gains[:, 12, :], A["final_norm"].rearrange(per_k, k=K)),
                     (bias_u[:], A["a_b_in"][0].rearrange("(a n p c) -> a p n c", a=2, p=P, c=2)[0])]
            for at, name in ((0, "norm_mix"), (2, "norm_ffn"), (5, "norm_ffn1_2"), (7, "norm_mix_2"), (9, "norm_ffn2_2")):
                small.append((gains[:, at:at + 2, :], A[name].rearrange("l (p k) -> p l k", k=K)))
            for l in range(LAYERS):
                small += [(router[:, l], A["moe_router"][l].rearrange("(p k) e -> p k e", k=K)),
                          (rbias[:, l, :], A["moe_bias"][l].partition_broadcast(P)),
                          (convb[:, l, :], A["conv_b_2"][l].rearrange("(a p) -> p a", p=P)),
                          (lam[:, l, :], A["lru_lambda_2"][l].rearrange("(a p) -> p a", p=P)),
                          (ba[:, l, :], A["lru_b_a_2"][l].rearrange("a p -> p a")),
                          (bx[:, l, :], A["lru_b_x_2"][l].rearrange("a p -> p a")),
                          (poolb[:, l, :], A["pool_b_2"][l].rearrange("a p -> p a")),
                          (pools[:, l, :], A["pool_scale_2"][l].rearrange("(a p) -> p a", p=P))]
                small += [(convw[:, l, j, :], A["conv_w_2"][l, j].rearrange("(a p) -> p a", p=P)) for j in range(CONV)]
            for dst, src in gm:
                eng.dma_start(dst, src).then_inc(gm_in, 16)
            for dst, src in small:
                eng.dma_start(dst, src, allow_slow_non_contiguous=True).then_inc(small_in, 16)
            small_total.append(16 * len(small))
            eng.wait_ge(c_in, 16)
            eng.activation(cact[:], cvec[:], ACT.Silu).then_inc(cact_ready, 1)
            norm_squares(0)
            eng.wait_ge(soft_a, 1)
            eng.activation(sp[:, 1], sp[:, 0], ACT.Exp, scale=-1.0).then_inc(soft_b, 1)
            round_h(h)
            next_hi(SPLIT)
            eng.dma_start(lng, A["a_ln_g"][0].partition_broadcast(P)).then_inc(ln_in, 16)
            eng.dma_start(lnb, A["a_ln_b"][0].partition_broadcast(P)).then_inc(ln_in, 16)

            for f in range(16):
                bk = pair_bank(f)
                wait_done(eng, b.at["unit", "gm"] + f)
                if f == 9:
                    eng.wait_ge(var_ready, 1)
                    eng.activation(stat[:, 50:55:4], stat[:, 49:54:4], ACT.Sqrt, bias=eps[:, 1:2]).then_inc(std_ready, 1)
                if f < 8:
                    eng.activation(vtok[:, :, f * W:(f + 1) * W], bank[bk][:], ACT.Gelu_apprx_tanh)\
                       .then_inc(drained[bk], 1)
                else:
                    g = f - 8
                    if g == 0:
                        eng.wait_ge(small_in, small_total[0])
                    eng.activation(ut[:, 2 * g, :], bank[bk][:, 0, :], ACT.Gelu_apprx_tanh, bias=bias_u[:, g, 0:1])
                    eng.activation(ut[:, 2 * g + 1, :], bank[bk][:, 1, :], ACT.Gelu_apprx_tanh,
                                   bias=bias_u[:, g, 1:2]).then_inc(drained[bk], 1)
                next_hi()
            next_hi(CHUNK_GROUPS - 1)

            for m in range(2):
                norm_squares(1 if m == 0 else 3)
                round_h(h)
                next_hi()
                wait_full(eng, "M", f"moe{m}scores")
                eng.activation(score, bank["M"][:, 0, 0:TT * E].rearrange("p (t e) -> p t e", t=TT), ACT.Sigmoid)\
                   .then_inc(drained["M"], 1)
                swiglu(f"moe{m}", E + 1)
                if m == 0:
                    norm_squares(2)
                    round_h(h)
                    next_hi()
                    for f in range(12):
                        if f == 4:
                            round_h(hkv, b.at["unit", "at"] + 3)
                        bk = pair_bank(f)
                        wait_done(eng, b.at["unit", "at"] + f)
                        dst = (qt_, kt_)[f // 4][:, 2 * (f % 4):2 * (f % 4) + 2, :] if f < 8 \
                            else va[:, :, (f - 8) * W:(f - 7) * W]
                        eng.activation(dst, bank[bk][:], ACT.Copy).then_inc(drained[bk], 1)
                        next_hi()

                    def turned(hd):
                        wait_full(eng, "B", "heads", hd)
                        eng.activation(pt[:, hd % 2, :], bank["B"][:].rearrange("p a s -> p (a s)")[:, 0:384], ACT.Copy)\
                           .then_inc(drained["B"], 1)

                    def heads_out(pair):
                        wait_full(eng, "M", "heads", pair)
                        eng.activation(ot[:, pair, :], bank["M"][:, 0, :], ACT.Copy).then_inc(drained["M"], 1)

                    for hd in range(HEADS):
                        eng.wait_ge(nmax_ready, hd + 1)
                        eng.activation(prob[:, hd % 2, 0, 0:P], smx[:, hd % 2, 0, 0:P], ACT.Exp,
                                       bias=nmax[:, hd % 2, 2:3], accum_out=nmax[:, hd % 2, 4:5])
                        eng.activation(prob[:, hd % 2, 1, :], smx[:, hd % 2, 1, :], ACT.Exp,
                                       bias=nmax[:, hd % 2, 3:4], accum_out=nmax[:, hd % 2, 5:6]).then_inc(exp_done, 1)
                        if hd >= 1:
                            turned(hd - 1)
                        if hd >= 3 and hd % 2:
                            heads_out((hd - 3) // 2)
                    turned(HEADS - 1)
                    heads_out(HEADS // 2 - 1)
                    next_hi(3)

            norm_squares(4)
            for l in range(LAYERS):
                norm_squares(5 + 3 * l)
                round_h(h)
                next_hi()
                eng.dma_start(wa, A["lru_w_a_2"][l].rearrange("a d e -> d a e")).then_inc(lru_in, 16)
                eng.dma_start(wx, A["lru_w_x_2"][l].rearrange("a d e -> d a e")).then_inc(lru_in, 16)
                eng.dma_start(poolw[:], A["pool_w_2"][l].rearrange("a d e -> d a e")).then_inc(lru_in, 16)
                swiglu(f"ffn1_{l}", FF_UNITS)
                norm_squares(6 + 3 * l)
                round_h(h)
                next_hi()
                for f in range(12):
                    bk = pair_bank(f)
                    wait_done(eng, b.at["unit", f"mix_{l}"] + f)
                    if f < 2:
                        eng.activation(pl0[:, 2 * f:2 * f + 2, PADP:], bank[bk][:], ACT.Copy).then_inc(drained[bk], 1)
                    elif f < 7:
                        g = 2 * (f - 2)
                        eng.activation(u_lru[:, g:g + 2, PADC:], bank[bk][:], ACT.Copy).then_inc(drained[bk], 1)
                    else:
                        g = 2 * (f - 7)
                        eng.activation(gl[:, g:g + 2, :], bank[bk][:], ACT.Gelu_apprx_tanh).then_inc(drained[bk], 1)
                    next_hi()
                for hd in range(LH):
                    bk = pair_bank(hd)
                    wait_pair_full(eng, f"gates_{l}", hd)
                    eng.activation(ra[:, hd, :], bank[bk][:, 0, :], ACT.Sigmoid, bias=ba[:, l, hd:hd + 1])\
                       .then_inc(act_step, 1)
                    eng.activation(ia[:, hd, :], bank[bk][:, 1, :], ACT.Sigmoid, bias=bx[:, l, hd:hd + 1])\
                       .then_inc(drained[bk], 1)
                next_hi()
                eng.wait_ge(act_step, LH * (2 * l + 1))
                eng.wait_ge(soft_c, 1)
                for hd in range(LH):
                    eng.activation(tl[:, hd, :], ra[:, hd, :], ACT.Tanh, scale=sp[:, 0, l, hd:hd + 1])\
                       .then_inc(act_step, 1)
                next_hi()
                eng.wait_ge(act_step, LH * (2 * l + 2))
                for hd in range(LH):
                    last = eng.activation(ra[:, hd, :], ra[:, hd, :], ACT.Exp, scale=sp[:, 1, l, hd:hd + 1])
                last.then_inc(decay_ready, 1)
                next_hi(2)
                for part, dst in enumerate((gpool, glru)):
                    wait_done(eng, b.at["unit", f"mix_{l}"] + 12 + 4 * part + 3)
                    for j in range(4):
                        last = eng.activation(dst[:, 2 * j:2 * j + 2, :], Y[:, 2 * j:2 * j + 2, :], ACT.Sigmoid)
                    last.then_inc(drained["Y"], 1)
                    if part == 0:
                        eng.wait_ge(square_ready, l + 1)
                        eng.activation(tl, tl, ACT.Sqrt).then_inc(root_ready, 1)
                    next_hi(4)
                next_hi(2 + 5 + 4 - 4 - 1)
                norm_squares(7 + 3 * l)
                round_h(h)
                next_hi()
                swiglu(f"ffn2_{l}", FF_UNITS)
            norm_squares(11)

        @block.tensor
        def _(eng):
            mm = eng.matmul

            def wait_unit(n, turn=0):
                eng.wait_ge(lo_ready, turn * PER_TURN + (n + 1))
                return part_hi[:, n % SPLIT, :], part_lo[:, n % SPLIT, :]

            def exact(out, w, x, start, stop, **more):
                mm(out, lhsT=w[0], rhs=x[0], start=start, stop=False, **more)
                mm(out, lhsT=w[0], rhs=x[1], start=False, stop=False, **more)
                return mm(out, lhsT=w[1], rhs=x[0], start=False, stop=stop, **more)

            def up_matmuls(parts, bk, stride2, ready=None):
                u = [view_a(p) for p in parts]
                for c in range(2):
                    cs = slice(c, None, 2) if stride2 else slice(c * P, (c + 1) * P)
                    for k in range(K):
                        if ready is not None and c == 0:
                            eng.wait_ge(h_ready, ready + k + 1)
                        last = exact(bank[bk][:, c, :], [v[:, k, cs] for v in u], (h_hi[:, k, :], h_lo[:, k, :]),
                                     k == 0, k == K - 1)
                last.then_inc(unit_done, 1)

            def rows_matmuls(parts, bk, bias=None, ready=None):
                u = [view_a(p) for p in parts]
                for t in range(TT):
                    ts = slice(t * P, (t + 1) * P)
                    if bias is not None:
                        mm(bank[bk][:, t, :], lhsT=ones[0:1, :], rhs=bias, start=True, stop=False)
                    for k in range(K):
                        if ready is not None and t == 0:
                            eng.wait_ge(h_ready, ready + k + 1)
                        last = exact(bank[bk][:, t, :], (h_hi[:, k, ts], h_lo[:, k, ts]), [v[:, k, :] for v in u],
                                     bias is None and k == 0, k == K - 1)
                last.then_inc(unit_done, 1)

            def down_matmuls(parts, rhs, first, end):
                u = [view_b(p) for p in parts]
                for j in range(K):
                    for c in range(2):
                        last = exact(Y[:, j, :], [v[:, c, j::K] for v in u], rhs(c), first and c == 0 and j % 2 == 0,
                                     end and c == 1, skip_group_check=True)
                last.then_inc(unit_done, 1)

            def split_rows(n, turn=0):
                eng.wait_ge(rows_ready, turn * GROUPS_PER_TURN + (n + 1))
                return lambda c: (rows_hi[:, n % 2, c, :], rows_lo[:, n % 2, c, :])

            def h_rows(q):
                return lambda c: (h_hi[:, 2 * q + c, :], h_lo[:, 2 * q + c, :])

            def norm_sum(n):
                key = "norm_" + NORMS[n]
                wait_free(eng, "B", key)
                for k in range(K):
                    if k % 2 == 0:
                        eng.wait_ge(sq_ready, 4 * n + k // 2 + 1)
                    last = mm(bank["B"][:, 0, :], lhsT=ones[:], rhs=h[:, k, :], start=(k == 0), stop=(k == K - 1))
                last.then_inc(filled["B"], 1)

            def swiglu(key, groups, expert0, ready, between=None, ahead=None):
                unit0 = b.at["unit", key]

                def up_part(n, turn=0, rdy=None):
                    for q, bk in enumerate("GU"):
                        parts = wait_unit(unit0 + max(3 * n - 1, 0) + q, turn)
                        wait_free(eng, bk, key, turn * GROUPS_PER_TURN + n)
                        up_matmuls(parts, bk, True, rdy if q == 0 else None)

                def gate_part(n, turn=0):
                    eng.wait_ge(row_ready, turn * GROUPS_PER_TURN + (expert0 + n))
                    wait_free(eng, "B", key, turn * GROUPS_PER_TURN + (n - 1))
                    mm(bank["B"][:, 0, :], lhsT=ones[0:E, :], rhs=gate_row[:, n % 2, :], start=True, stop=True)\
                        .then_inc(filled["B"], 1)

                def down_part(n, turn=0, end=False):
                    parts = wait_unit(unit0 + 3 * n + 4 - end * 2, turn)
                    down_matmuls(parts, split_rows(b.at["down", key] + n, turn), n == 0, end)

                def group(n, turn=0):
                    up_part(n, turn)
                    if expert0 is not None:
                        gate_part(n, turn)
                    down_part(n - 1, turn)

                up_part(0, rdy=ready)
                if between:
                    between()
                group(1)
                turns = (groups - 2) // GROUPS_PER_TURN
                with eng.Fori(0, turns) as i:
                    for g in range(GROUPS_PER_TURN):
                        group(2 + g, i)
                for n in range(2 + turns * GROUPS_PER_TURN, groups):
                    group(n)
                if ahead:
                    ahead()
                down_part(groups - 1, end=True)

            eng.wait_ge(consts, 1)
            eng.wait_ge(x_in, 16)
            for f in range(4):
                bk = pair_bank(f)
                wait_pair_free(eng, "x", f)
                for j in range(4):
                    k, t = 2 * f + j // 2, j % 2
                    last = eng.transpose(bank[bk][:, j // 2, t * P:(t + 1) * P], xtok[:, t, k::K], ident[:])
                last.then_inc(filled[bk], 1)
            norm_sum(0)
            def ada_fill(fill):
                a, z = FILLS[fill]
                wait_free(eng, "M", fill)
                for i in range(a, z):
                    eng.wait_ge(ada_ready, i + 1)
                    for j in range(K):
                        col = VECTORS[i] * K + j
                        last = mm(bank["M"][:, 0, col:col + 1], lhsT=share(i)[:, j::K], rhs=ones[:, 0:1],
                                  start=(i == a and j == 0), stop=True, skip_group_check=True)
                last.then_inc(filled["M"], 1)

            eng.wait_ge(consts, 2)
            for f in range(2):
                bk = pair_bank(f)
                wait_pair_free(eng, "ws", f)
                for j in range(4):
                    last = eng.transpose(bank[bk][:, j // 2, (j % 2) * P:(j % 2 + 1) * P], ws[:, 4 * f + j, :], ident[:])
                last.then_inc(filled[bk], 1)

            ada_fill("ada_first")

            eng.wait_ge(gm_in, 16 * 3)

            def sv(g):
                bk = pair_bank(g)
                wait_pair_free(eng, "sv", g)
                for c in range(2):
                    for t in range(TT):
                        o = bank[bk][:, c, t * P:(t + 1) * P]
                        mm(o, lhsT=vtok[:, t, g * W + c:(g + 1) * W:2], rhs=wst[:, g, :], start=True, stop=False)
                        last = mm(o, lhsT=ones[0:1, :], rhs=bs_row[0:1, g * P:(g + 1) * P], start=False, stop=True)
                last.then_inc(filled[bk], 1)

            for n in range(GM_UNITS):
                if n < 16:
                    parts = wait_unit(n)
                    wait_pair_free(eng, "gm_in", n)
                    if n < 8:
                        rows_matmuls(parts, pair_bank(n), bv_row[0:1, n * W:(n + 1) * W], 0 if n == 0 else None)
                    else:
                        up_matmuls(parts, pair_bank(n), True)
                else:
                    g = n - 16
                    if g == 0:
                        eng.wait_ge(gv_ready, 1)
                        sv(0)
                    if g + 1 < CHUNK_GROUPS:
                        sv(g + 1)
                    down_matmuls(wait_unit(n), split_rows(g), g == 0, g == 7)
                if n == 21:
                    ada_fill("ada_gm")
            ada_fill("ada_ffn")

            for m in range(2):
                key = f"moe{m}"
                norm_sum(1 + 2 * m)
                raw = K * (1 if m == 0 else 4)
                wait_free(eng, "M", key + "scores")
                if m == 0:
                    eng.wait_ge(small_in, small_total[0])
                for t in range(TT):
                    for k in range(K):
                        if t == 0:
                            eng.wait_ge(raw_ready, raw + k + 1)
                        last = mm(bank["M"][:, 0, t * E:(t + 1) * E], lhsT=h[:, k, t * P:(t + 1) * P],
                                  rhs=router[:, m, k, :], start=(k == 0), stop=(k == K - 1))
                last.then_inc(filled["M"], 1)

                def turn_weights():
                    eng.wait_ge(weights_ready, m + 1)
                    wait_free(eng, "M", key + "weights")
                    for t in range(TT):
                        last = eng.transpose(bank["M"][0:E, 0, t * P:(t + 1) * P], wtok[:, t, :], ident[:])
                    last.then_inc(filled["M"], 1)

                swiglu(key, E + 1, E * m, raw, turn_weights, (lambda: ada_fill("ada_moe")) if m == 0 else None)
                if m == 1:
                    break
                ada_fill("ada_at")
                norm_sum(2)
                ada_fill("ada_last")
                at0 = b.at["unit", "at"]
                for f in range(12):
                    parts = wait_unit(at0 + f)
                    wait_pair_free(eng, "qkv", f)
                    if f < 8:
                        up_matmuls(parts, pair_bank(f), False, {0: 2 * K, 4: 3 * K}.get(f))
                    else:
                        rows_matmuls(parts, pair_bank(f))
                for f in range(12):
                    wait_pair_drained(eng, "qkv", f)

                def scores(hd):
                    bk, ch, p0 = pair_bank(hd), hd // 2, DH * (hd % 2)
                    wait_pair_free(eng, "heads", hd)
                    for t in range(TT):
                        last = mm(bank[bk][:, t, :], lhsT=qt_[p0:p0 + DH, ch, t * P:(t + 1) * P],
                                  rhs=kt_[p0:p0 + DH, ch, :], start=True, stop=True)
                    last.then_inc(filled[bk], 1)

                def turn(hd):
                    eng.wait_ge(prob_ready, hd + 1)
                    wait_free(eng, "B", "heads", hd)
                    o = bank["B"][:].rearrange("p a s -> p (a s)")
                    pr = prob[:, hd % 2]
                    eng.transpose(o[:, 0:P], pr[:, 0, 0:P], ident[:])
                    eng.transpose(o[:, P:2 * P], pr[:, 1, 0:P], ident[:])
                    eng.transpose(o[:, 2 * P:3 * P], pr[:, 1, P:2 * P], ident[:]).then_inc(filled["B"], 1)

                def values(hd):
                    ch, p0 = hd // 2, DH * (hd % 2)
                    wait_drained(eng, "B", "heads", hd)
                    if hd % 2 == 0:
                        wait_free(eng, "M", "heads", hd // 2)
                    o = bank["M"][p0:p0 + DH, 0, :]
                    mm(o, lhsT=va[:, 0, hd * DH:(hd + 1) * DH], rhs=pt[:, hd % 2, 0:S], start=True, stop=False,
                       skip_group_check=True)
                    last = mm(o[:, P:S], lhsT=va[:, 1, hd * DH:(hd + 1) * DH], rhs=pt[:, hd % 2, S:S + P], start=False,
                              stop=True, skip_group_check=True)
                    if hd % 2:
                        last.then_inc(filled["M"], 1)

                scores(0)
                scores(1)
                for hd in range(HEADS):
                    if hd + 2 < HEADS:
                        scores(hd + 2)
                    turn(hd)
                    if hd >= 1:
                        values(hd - 1)
                values(HEADS - 1)
                for q in range(4):
                    down_matmuls(wait_unit(at0 + 12 + q), split_rows(b.at["down", "at"] + q), q == 0, q == 3)

            norm_sum(4)
            for l in range(LAYERS):
                norm_sum(5 + 3 * l)
                swiglu(f"ffn1_{l}", FF_UNITS, None, K * (5 + 3 * l))
                norm_sum(6 + 3 * l)
                unit = b.at["unit", f"mix_{l}"]
                for f in range(12):
                    parts = wait_unit(unit + f)
                    wait_pair_free(eng, f"in_{l}", f)
                    up_matmuls(parts, pair_bank(f), False, K * (6 + 3 * l) if f == 0 else None)
                eng.wait_ge(lru_in, 48 * (l + 1))
                for f in range(2):
                    wait_free(eng, "M", f"pool_{l}", f)
                    eng.wait_ge(pooled_ready, l + 1)
                    for c in range(2):
                        g = 2 * f + c
                        last = mm(bank["M"][:, c, :], lhsT=poolw[:, g, :], rhs=pools_of(g), start=True, stop=True)
                    last.then_inc(filled["M"], 1)
                for hd in range(LH):
                    bk = pair_bank(hd)
                    eng.wait_ge(conv_ready, LH * l + hd + 1)
                    wait_pair_free(eng, f"gates_{l}", hd)
                    mm(bank[bk][:, 0, :], lhsT=wa[:, hd, :], rhs=vconv[:, hd, :], start=True, stop=True)
                    mm(bank[bk][:, 1, :], lhsT=wx[:, hd, :], rhs=vconv[:, hd, :], start=True, stop=True)\
                        .then_inc(filled[bk], 1)
                for part in range(2):
                    if part:
                        wait_drained(eng, "Y", f"gp_{l}")
                    for q in range(4):
                        down_matmuls(wait_unit(unit + 12 + 4 * part + q), h_rows(q), q == 0, q == 3)
                wait_drained(eng, "Y", f"gl_{l}")
                down = b.at["down", f"mix_{l}"]
                for q in range(POOL_UNITS):
                    down_matmuls(wait_unit(unit + 20 + q), split_rows(down + q), q == 0, q == POOL_UNITS - 1)
                wait_drained(eng, "Y", f"yp_{l}")
                for q in range(LRU_UNITS):
                    down_matmuls(wait_unit(unit + 22 + q), split_rows(down + 2 + q), q == 0, q == LRU_UNITS - 1)
                wait_drained(eng, "Y", f"yl_{l}")
                for q in range(4):
                    down_matmuls(wait_unit(unit + 27 + q), split_rows(down + 7 + q), q == 0, q == 3)
                norm_sum(7 + 3 * l)
                swiglu(f"ffn2_{l}", FF_UNITS, None, K * (7 + 3 * l))
            norm_sum(11)
            eng.wait_ge(h_ready, K * 12)
            for f in range(4):
                bk, t = pair_bank(f), f // 2
                wait_pair_free(eng, "final", f)
                for j in range(4):
                    k = 4 * (f % 2) + j
                    last = eng.transpose(bank[bk][:, j // 2, (j % 2) * P:(j % 2 + 1) * P], h[:, k, t * P:(t + 1) * P],
                                         ident[:])
                last.then_inc(filled[bk], 1)

        @block.vector
        def _(eng):
            steps = [0]

            def link(ins):
                steps[0] += 1
                ins.then_inc(dve_step, 1)
                eng.wait_ge(dve_step, steps[0])

            def mark(ins):
                steps[0] += 1
                ins.then_inc(dve_step, 1)
                return steps[0]

            def add_share(n):
                at = order.index(("ada", n))
                eng.wait_ge(landed[at % RING], 16 * (at // RING + 1))
                u = view_b(ring[:, at % RING, :])
                dst, q = share(n // 4), n % 4
                for c in range(2):
                    if q == 0 and c == 0:
                        o = eng.tensor_scalar(dst, u[:, 0, :], cact[:, 0:1], None, ALU.mult)
                    else:
                        eng.wait_ge(ada_step, shares[0])
                        o = eng.scalar_tensor_tensor(out=dst, in0=u[:, c, :], scalar=cact[:, 2 * q + c:2 * q + c + 1], in1=dst,
                                                     op0=ALU.mult, op1=ALU.add)
                    if c == 0 or q < 3:
                        o.then_inc(ada_step, 1)
                        shares[0] += 1
                    else:
                        o.then_inc(ada_ready, 1)

            split_off, shares = [0], [0]

            def next_lo(count=1, turn=0):
                for _ in range(count):
                    n = split_off[0]
                    split_off[0] += 1
                    if n >= b.n["unit"]:
                        continue
                    slot, _ = arrival(n)
                    eng.wait_ge(hi_ready, turn * PER_TURN + (n + 1))
                    eng.tensor_tensor(part_lo[:, n % SPLIT, :], ring[:, slot, :], part_hi[:, n % SPLIT, :].bitcast(F32),
                                      ALU.subtract).then_inc(lo_ready, 1)
                    if n < 2 * ADA_MORE and n % 2 == 0:
                        add_share(ADA_FIRST + n // 2)

            def split(src, n, read=None, turn=0):
                if read is not None:
                    wait_done(eng, read, turn)
                hi = rows_hi[:, n % 2]
                eng.tensor_copy(hi, src).then_inc(rows_round, 1)
                eng.wait_ge(rows_round, turn * GROUPS_PER_TURN + (n + 1))
                eng.tensor_tensor(rows_lo[:, n % 2], src, hi.bitcast(F32), ALU.subtract).then_inc(rows_ready, 1)

            hs = [0]

            def chunk_lo(src, k):
                eng.wait_ge(h_round, hs[0] + k + 1)
                eng.tensor_tensor(h_lo[:, k, :], src[:, k, :], h_hi[:, k, :].bitcast(F32), ALU.subtract).then_inc(h_ready, 1)

            def norm(n, outs):
                key = "norm_" + NORMS[n]
                wait_drained(eng, "B", key)
                link(eng.reciprocal(rstd[:], rstd[:]))
                for dst, gain, shift, ready in outs:
                    scaled = []
                    splits = ready is raw_ready and dst is h
                    for k in range(K + 3):
                        if k < K:
                            o = eng.scalar_tensor_tensor(out=dst[:, k, :], in0=x[:, k, :], scalar=gain[:, k:k + 1],
                                                         in1=rstd[:], op0=ALU.mult, op1=ALU.mult)
                            if shift is not None:
                                scaled.append(mark(o))
                            elif ready is not x_ready or k % 2:
                                o.then_inc(ready, 1)
                        if shift is not None and 0 <= k - 1 < K:
                            eng.wait_ge(dve_step, scaled[k - 1])
                            eng.tensor_scalar(dst[:, k - 1, :], dst[:, k - 1, :], shift[:, k - 1:k], None, ALU.add)\
                               .then_inc(ready, 1)
                        if splits and 0 <= k - 3 < K:
                            chunk_lo(dst, k - 3)
                    if splits:
                        hs[0] += K
                if outs[0][3] is x_ready:
                    eng.wait_ge(x_ready, 4 * (n + 1))

            def update(u, last_unit, gain):
                wait_done(eng, last_unit)
                for j in range(4):
                    if isinstance(gain, float):
                        o = eng.scalar_tensor_tensor(out=x[:, 2 * j:2 * j + 2, :], in0=Y[:, 2 * j:2 * j + 2, :], scalar=gain,
                                                     in1=x[:, 2 * j:2 * j + 2, :], op0=ALU.mult, op1=ALU.add)
                    else:
                        for c in (2 * j, 2 * j + 1):
                            o = eng.scalar_tensor_tensor(out=x[:, c, :], in0=Y[:, c, :], scalar=gain[:, c:c + 1],
                                                         in1=x[:, c, :], op0=ALU.mult, op1=ALU.add)
                    o.then_inc(x_ready, 1)
                eng.wait_ge(x_ready, 4 * (u + 1))

            def hidden_group(key, n, expert=None, turn=0):
                i4 = turn * GROUPS_PER_TURN
                if expert is not None:
                    eng.tensor_scalar(gate_row[:, n % 2, :], wt[:], ident[0:E, bass.ds(expert, 1)], None, ALU.mult)\
                       .then_inc(row_ready, 1)
                next_lo(1, turn)
                wait_drained(eng, "G", key, i4 + n)
                wait_done(eng, b.at["unit", key] + max(3 * n, 1), turn)
                eng.wait_ge(rows_ready, i4 + (b.at["down", key] + n))
                eng.tensor_tensor(hidden, silu, bank["U"][:], ALU.mult).then_inc(drained["U"], 1)
                wait_drained(eng, "U", key, i4 + n)
                if expert is not None:
                    wait_full(eng, "B", key, i4 + (n - 1))
                    eng.tensor_tensor(hidden, hidden, bank["B"][:, 0:1, :].broadcast_to([P, 2, S]), ALU.mult)\
                       .then_inc(drained["B"], 1)
                    wait_drained(eng, "B", key, i4 + (n - 1))
                split(hidden, b.at["down", key] + n, None, turn)
                next_lo(1 if n == 0 else 2, turn)

            def swiglu(key, groups, gated):
                turns = (groups - 2) // GROUPS_PER_TURN
                hidden_group(key, 1, 0 if gated else None)
                with eng.Fori(0, turns) as i:
                    for g in range(GROUPS_PER_TURN):
                        hidden_group(key, 2 + g, i * GROUPS_PER_TURN + (1 + g) if gated else None, i)
                split_off[0] += (turns - 1) * PER_TURN
                for n in range(2 + turns * GROUPS_PER_TURN, groups):
                    hidden_group(key, n, n - 1 if gated else None)

            for f in range(4):
                bk = pair_bank(f)
                wait_pair_full(eng, "x", f)
                eng.tensor_copy(x[:, 2 * f:2 * f + 2, :], bank[bk][:]).then_inc(drained[bk], 1)
            for f in range(2):
                bk = pair_bank(f)
                wait_pair_full(eng, "ws", f)
                eng.tensor_copy(wst[:, 4 * f:4 * f + 4, :], bank[bk][:].rearrange("p a (g s) -> p (a g) s", g=2))\
                   .then_inc(drained[bk], 1)
            eng.wait_ge(cact_ready, 1)
            for n in range(ADA_FIRST):
                add_share(n)
            eng.wait_ge(small_in, small_total[0])
            eng.scalar_tensor_tensor(out=sp[:, 0], in0=lam[:], scalar=-1.0, in1=lam[:], op0=ALU.mult, op1=ALU.max)\
               .then_inc(soft_a, 1)
            def vec(v):
                return ada[:, v * K:(v + 1) * K]

            def coefficient(at, gain, scale):
                link(eng.scalar_tensor_tensor(out=coef[:, at, :], in0=vec(scale), scalar=1.0, in1=gains[:, gain, :],
                                              op0=ALU.add, op1=ALU.mult))

            def modulation(fill):
                wait_full(eng, "M", fill)
                vs = sorted(VECTORS[slice(*FILLS[fill])])
                runs = [v for v in vs if v - 1 not in vs]
                for v in runs:
                    z = v
                    while z in vs:
                        z += 1
                    o = eng.tensor_tensor(ada[:, v * K:z * K], bank["M"][:, 0, v * K:z * K], adab[:, v * K:z * K], ALU.add)
                o.then_inc(drained["M"], 1)
                wait_drained(eng, "M", fill)

            modulation("ada_first")
            coefficient(0, 0, 1)
            norm(0, [(h, coef[:, 0], vec(0), raw_ready)])
            next_lo(SPLIT)
            eng.wait_ge(soft_b, 1)
            link(eng.tensor_scalar(sp[:, 2], sp[:, 1], 2.0, None, ALU.add))
            link(eng.reciprocal(sp[:, 2], sp[:, 2]))
            link(eng.tensor_tensor(sp[:, 2], sp[:, 2], sp[:, 1], ALU.mult))
            link(eng.tensor_tensor(sp[:, 3], sp[:, 2], sp[:, 2], ALU.mult))
            link(eng.tensor_scalar(sp[:, 4], sp[:, 3], 1.0 / 17, None, ALU.mult))
            for m in (15, 13, 11, 9, 7, 5, 3):
                link(eng.scalar_tensor_tensor(out=sp[:, 4], in0=sp[:, 4], scalar=1.0 / m, in1=sp[:, 3],
                                              op0=ALU.add, op1=ALU.mult))
            link(eng.scalar_tensor_tensor(out=sp[:, 4], in0=sp[:, 4], scalar=1.0, in1=sp[:, 2], op0=ALU.add, op1=ALU.mult))
            link(eng.tensor_scalar(sp[:, 3], lam[:], -1.0, 0.0, ALU.mult, ALU.max))
            link(eng.scalar_tensor_tensor(out=sp[:, 4], in0=sp[:, 4], scalar=2.0, in1=sp[:, 3], op0=ALU.mult, op1=ALU.add))
            eng.tensor_scalar(sp[:, 0], sp[:, 4], 8.0, None, ALU.mult)
            eng.tensor_scalar(sp[:, 1], sp[:, 4], -8.0, None, ALU.mult).then_inc(soft_c, 1)

            next_lo(8)

            eng.wait_ge(ln_in, 16 * 2)
            for f in range(8):
                wait_pair_drained(eng, "gm_in", f)
            st = stat[:, 0:48].rearrange("p (t n s) -> p t n s", t=TT, n=4)
            for t in range(TT):
                for n in range(4):
                    s = mark(eng.bn_stats(st[:, t, n, :], vtok[:, t, n * 512:(n + 1) * 512]))
            eng.wait_ge(dve_step, s)
            for t in range(TT):
                o = eng.bn_aggr(stat[:, 48 + 4 * t:50 + 4 * t], st[:, t].rearrange("p n s -> p (n s)"))
            o.then_inc(var_ready, 1)
            eng.wait_ge(std_ready, 1)
            for t in range(TT):
                mv = stat[:, 48 + 4 * t:52 + 4 * t]
                link(eng.reciprocal(mv[:, 3:4], mv[:, 2:3]))
                link(eng.tensor_scalar(vtok[:, t, :], vtok[:, t, :], mv[:, 0:1], mv[:, 3:4], ALU.subtract, ALU.mult))
                link(eng.tensor_tensor(vtok[:, t, :], vtok[:, t, :], lng, ALU.mult))
                o = eng.tensor_tensor(vtok[:, t, :], vtok[:, t, :], lnb, ALU.add)
            o.then_inc(gv_ready, 1)
            next_lo(7)
            for g in range(CHUNK_GROUPS):
                bk = pair_bank(g)
                wait_pair_drained(eng, "gm_in", 8 + g)
                wait_pair_full(eng, "sv", g)
                uu = ut[:, 2 * g:2 * g + 2, :]
                eng.tensor_tensor(uu, uu, bank[bk][:], ALU.mult).then_inc(drained[bk], 1)
                wait_pair_drained(eng, "sv", g)
                split(uu, g, 16 + g - 2 if g >= 2 else None)
                if g:
                    next_lo()
            next_lo()
            modulation("ada_gm")
            update(0, GM_UNITS - 1, vec(2))
            modulation("ada_ffn")
            coefficient(1, 2, 4)

            for m in range(2):
                key = f"moe{m}"
                norm(1 + 2 * m, [(h, coef[:, 1 + 2 * m], vec(3 + 6 * m), raw_ready)])
                next_lo()
                link(eng.memset(grp12[:, :, 8:12], TOP))
                wait_drained(eng, "M", key + "scores")
                link(eng.tensor_tensor(choice, score, rbias[:, m:m + 1, :].broadcast_to([P, TT, E]), ALU.add))
                for t in range(TT):
                    for g in range(EG):
                        s = mark(eng.max(best8[:, t, g, :], choice[:, t, g * 8:(g + 1) * 8]))
                eng.wait_ge(dve_step, s)
                link(eng.tensor_tensor(grp12[:, :, 0:8], best8[:, :, :, 0], best8[:, :, :, 1], ALU.add))
                for t in range(TT):
                    link(eng.max(grp8[:, t, :], grp12[:, t, :]))
                    link(eng.match_replace(grpt[:, t, :], grp8[:, t, :], grp12[:, t, :], GONE))
                link(eng.tensor_scalar(gmask, grpt[:, :, 0:8], GONE, None, ALU.is_equal))
                link(eng.tensor_scalar(goff, gmask, -1.0, -NEG, ALU.add, ALU.mult))
                for t in range(TT):
                    cv = choice[:, t, :].rearrange("p (g e) -> p g e", g=EG)
                    link(eng.tensor_tensor(cv, cv, gmask[:, t, :].unsqueeze(2).broadcast_to([P, EG, 8]), ALU.mult))
                    link(eng.tensor_tensor(cv, cv, goff[:, t, :].unsqueeze(2).broadcast_to([P, EG, 8]), ALU.add))
                    link(eng.max(top8[:, t, :], choice[:, t, :]))
                    link(eng.match_replace(taken[:, t, :], top8[:, t, :], choice[:, t, :], GONE))
                link(eng.tensor_scalar(taken, taken, GONE, None, ALU.is_equal))
                link(eng.tensor_tensor(wtok, score, taken, ALU.mult))
                link(eng.tensor_reduce(wsum, wtok, AX.X, ALU.add))
                link(eng.reciprocal(wsum, wsum))
                for t in range(TT):
                    o = eng.tensor_scalar(wtok[:, t, :], wtok[:, t, :], wsum[:, t:t + 1], ROUTED_SCALE, ALU.mult, ALU.mult)
                o.then_inc(weights_ready, 1)
                hidden_group(key, 0)
                wait_full(eng, "M", key + "weights")
                eng.tensor_copy(wt[:], bank["M"][0:E, 0, :]).then_inc(drained["M"], 1)
                wait_drained(eng, "M", key + "weights")
                swiglu(key, E + 1, True)
                if m == 0:
                    modulation("ada_moe")
                update(1 + 2 * m, b.at["unit", key] + 3 * E + 2, vec(5 + 6 * m))
                if m == 1:
                    break
                modulation("ada_at")
                coefficient(2, 1, 7)
                coefficient(4, 4, 13)
                norm(2, [(h, coef[:, 2], vec(6), raw_ready), (hkv, coef[:, 4], vec(12), raw_ready)])
                next_lo(5)
                wait_done(eng, b.at["unit", "at"] + 3)
                for k in range(K):
                    chunk_lo(hkv, k)
                hs[0] += K
                modulation("ada_last")
                coefficient(3, 3, 10)
                next_lo(8)

                def maxima(hd):
                    bk, q = pair_bank(hd), hd % 2
                    wait_pair_full(eng, "heads", hd)
                    eng.scalar_tensor_tensor(out=smx[:, q], in0=bank[bk][:], scalar=DH ** -0.5, in1=mask[:], op0=ALU.mult,
                                             op1=ALU.add).then_inc(drained[bk], 1)
                    wait_pair_drained(eng, "heads", hd)
                    link(eng.tensor_reduce(nmax[:, q, 0:2], smx[:, q], AX.X, ALU.max))
                    eng.tensor_scalar(nmax[:, q, 2:4], nmax[:, q, 0:2], -1.0, None, ALU.mult).then_inc(nmax_ready, 1)

                def normalise(hd):
                    q = hd % 2
                    eng.wait_ge(exp_done, hd + 1)
                    link(eng.reciprocal(nmax[:, q, 6:8], nmax[:, q, 4:6]))
                    eng.tensor_scalar(prob[:, q, 0, 0:P], prob[:, q, 0, 0:P], nmax[:, q, 6:7], None, ALU.mult)
                    eng.tensor_scalar(prob[:, q, 1, :], prob[:, q, 1, :], nmax[:, q, 7:8], None, ALU.mult)\
                       .then_inc(prob_ready, 1)

                maxima(0)
                maxima(1)
                for hd in range(HEADS):
                    normalise(hd)
                    if hd + 2 < HEADS:
                        maxima(hd + 2)
                for q in range(4):
                    wait_drained(eng, "M", "heads", 2 * q + 1)
                    split(ot[:, 2 * q:2 * q + 2, :], b.at["down", "at"] + q, b.at["unit", "at"] + 12 + q - 2 if q >= 2 else None)
                    if q:
                        next_lo()
                update(2, b.at["unit", "at"] + 15, vec(8))

            norm(4, [(x, gains[:, 12], None, x_ready)])
            for l in range(LAYERS):
                norm(5 + 3 * l, [(h, gains[:, 5 + l], None, raw_ready)])
                next_lo()
                hidden_group(f"ffn1_{l}", 0)
                swiglu(f"ffn1_{l}", FF_UNITS, False)
                update(5 + 3 * l, b.at["unit", f"ffn1_{l}"] + 3 * FF_UNITS - 1, 0.5)
                norm(6 + 3 * l, [(h, gains[:, 7 + l], None, raw_ready)])
                next_lo()
                for buf in (pl0, pl1, pl2):
                    link(eng.memset(buf[:, :, 0:PADP], 0.0))
                link(eng.memset(u_lru[:, :, 0:PADC], 0.0))
                next_lo(2)
                for f in range(2):
                    wait_pair_drained(eng, f"in_{l}", f)
                src = pl0
                for n in range(4):
                    dst = pl1 if n % 2 == 0 else pl2
                    w = 1 << n
                    link(eng.tensor_tensor(dst[:, n:4, PADP:], src[:, n:4, PADP:], src[:, n:4, PADP - w:PADP + S - w], ALU.add))
                    src = dst
                for g in range(4):
                    w = 2 << g
                    buf = pl1 if g % 2 == 0 else pl2
                    link(eng.tensor_tensor(buf[:, g, PADP:PADP + w - 1], buf[:, g, PADP:PADP + w - 1],
                                           inv_count[:, g, 0:w - 1], ALU.mult))
                    link(eng.tensor_scalar(buf[:, g, PADP + w - 1:], buf[:, g, PADP + w - 1:], 1.0 / w, None, ALU.mult))
                    o = eng.tensor_tensor(pools_of(g), pools_of(g), pl0[:, g, PADP:], ALU.subtract)
                o.then_inc(pooled_ready, 1)
                next_lo(2)
                for hd in range(LH):
                    if hd % 2 == 0:
                        wait_pair_drained(eng, f"in_{l}", 2 + hd // 2)
                        next_lo()
                    v = vconv[:, hd, :]
                    link(eng.tensor_scalar(v, u_lru[:, hd, PADC:], convw[:, l, CONV - 1, hd:hd + 1], convb[:, l, hd:hd + 1],
                                           ALU.mult, ALU.add))
                    for j in range(CONV - 1):
                        o = eng.scalar_tensor_tensor(out=v, in0=u_lru[:, hd, j:j + S], scalar=convw[:, l, j, hd:hd + 1], in1=v,
                                                     op0=ALU.mult, op1=ALU.add)
                        if j < CONV - 2:
                            link(o)
                    o.then_inc(conv_ready, 1)
                next_lo(3)
                unit, down = b.at["unit", f"mix_{l}"], b.at["down", f"mix_{l}"]
                for f in range(2):
                    wait_full(eng, "M", f"pool_{l}", f)
                    for c in range(2):
                        g = 2 * f + c
                        o = eng.tensor_scalar(mixed[:, g, :], bank["M"][:, c, :], poolb[:, l, g:g + 1], pools[:, l, g:g + 1],
                                              ALU.add, ALU.mult)
                    o.then_inc(drained["M"], 1)
                    wait_drained(eng, "M", f"pool_{l}", f)
                    split(mixed[:, 2 * f:2 * f + 2, :], down + f)
                next_lo(2)
                eng.wait_ge(decay_ready, l + 1)
                link(eng.tensor_tensor(ia, ia, vconv, ALU.mult))
                link(eng.tensor_scalar(vconv, tl, 1.0, None, ALU.add))
                next_lo()
                link(eng.reciprocal(vconv, vconv))
                eng.scalar_tensor_tensor(out=tl, in0=tl, scalar=2.0, in1=vconv, op0=ALU.mult, op1=ALU.mult)\
                   .then_inc(square_ready, 1)
                next_lo()
                eng.wait_ge(root_ready, l + 1)
                link(eng.tensor_tensor(ia, ia, tl, ALU.mult))
                for hd in range(LH):
                    if hd in (0, LH // 2):
                        next_lo()
                    s = mark(eng.tensor_tensor_scan(vconv[:, hd, :], ra[:, hd, :], ia[:, hd, :], 0.0, ALU.mult, ALU.add))
                eng.wait_ge(dve_step, s)
                for f in range(5):
                    wait_pair_drained(eng, f"in_{l}", 7 + f)
                link(eng.tensor_tensor(gl, gl, vconv, ALU.mult))
                next_lo(2)

                def gated(dst, last_unit):
                    wait_done(eng, last_unit)
                    for j in range(4):
                        o = eng.tensor_tensor(dst[:, 2 * j:2 * j + 2, :], dst[:, 2 * j:2 * j + 2, :],
                                              Y[:, 2 * j:2 * j + 2, :], ALU.mult)
                    o.then_inc(drained["Y"], 1)

                wait_drained(eng, "Y", f"gl_{l}")
                split(gl[:, 0:2, :], down + 2, unit + 20)
                next_lo()
                gated(gpool, unit + 21)
                split(gl[:, 2:4, :], down + 3, unit + 21)
                next_lo()
                for q in range(2, LRU_UNITS):
                    split(gl[:, 2 * q:2 * q + 2, :], down + 2 + q, unit + 22 + q - 2)
                    next_lo()
                gated(glru, unit + 26)
                wait_drained(eng, "Y", f"yl_{l}")
                link(eng.tensor_tensor(gpool[:], gpool[:], glru, ALU.add))
                split(gpool[:, 0:2, :], down + 7, unit + 25)
                split(gpool[:, 2:4, :], down + 8, unit + 26)
                next_lo(3)
                split(gpool[:, 4:6, :], down + 9, unit + 27)
                next_lo()
                split(gpool[:, 6:8, :], down + 10, unit + 28)
                next_lo()
                update(6 + 3 * l, b.at["unit", f"mix_{l}"] + 30, 1.0)
                norm(7 + 3 * l, [(h, gains[:, 9 + l], None, raw_ready)])
                next_lo()
                hidden_group(f"ffn2_{l}", 0)
                swiglu(f"ffn2_{l}", FF_UNITS, False)
                update(7 + 3 * l, b.at["unit", f"ffn2_{l}"] + 3 * FF_UNITS - 1, 0.5)
            norm(11, [(h, gains[:, 11], None, h_ready)])
            for f in range(4):
                bk, t = pair_bank(f), f // 2
                wait_pair_full(eng, "final", f)
                dst = otok[:, t, :].rearrange("p (w k) -> p k w", k=K)[:, 4 * (f % 2):4 * (f % 2) + 4, :]
                eng.tensor_copy(dst, bank[bk][:].rearrange("p a (g w) -> p (a g) w", g=2)).then_inc(drained[bk], 1)


_INS = [
    'x', 'c', 'ada_w', 'ada_b', 'norm_mix', 'norm_ffn', 'a_w_in', 'a_b_in', 'a_ln_g', 'a_ln_b', 'a_w_s', 'a_b_s',
    'a_w_out', 'kv_norm', 'kv_ada_w', 'kv_ada_b', 'kv_w_k', 'kv_w_v', 'b_w_q', 'b_w_o', 'moe_router', 'moe_bias',
    'moe_w_gate', 'moe_w_up', 'moe_w_down', 'sh_w_gate', 'sh_w_up', 'sh_w_down', 'final_norm', 'norm_ffn1_2',
    'ffn1_w_up_2', 'ffn1_w_down_2', 'norm_mix_2', 'w_in_2', 'pool_w_2', 'pool_b_2', 'pool_scale_2',
    'w_pool_up_2', 'conv_w_2', 'conv_b_2', 'lru_w_a_2', 'lru_b_a_2', 'lru_w_x_2', 'lru_b_x_2', 'lru_lambda_2',
    'w_lru_up_2', 'w_out_2', 'norm_ffn2_2', 'ffn2_w_up_2', 'ffn2_w_down_2', 'final_norm_2',
]


def kernel(**inputs):
    import numpy as _np
    import concourse.bacc as _bacc
    from concourse import mybir as _mybir
    from concourse.bass_utils import run_bass_kernel_spmd as _run

    nc = _bacc.Bacc("TRN2", target_bir_lowering=False, num_devices=1)
    arrays, args = {}, {}
    for name in _INS:
        a = _np.ascontiguousarray(inputs[name])
        arrays[f"in_{name}_dram"] = a
        args[name] = nc.dram_tensor(f"in_{name}_dram", a.shape, _mybir.dt.from_np(a.dtype), kind="ExternalInput").ap()
    out = nc.dram_tensor("out_0_dram", (1, S, D), F32, kind="ExternalOutput").ap()
    build(nc, args, out)
    r = _run(nc, [arrays], core_ids=[0])
    return r.results[0]["out_0_dram"]
```
